# Optimizing a Trainium2 kernel written in Bass

```python
import math
import jax, jax.numpy as jnp
from jax import lax
import numpy as np

D_MODEL = 2048
BATCH = 1
SEQ = 256
DEPTH = 1

N_ATT_HEADS = 8
HEAD_DIM = 128
ATT_WIDTH = N_ATT_HEADS * HEAD_DIM
DILATED_PATTERNS = ((128, 1), (512, 4), (2048, 16))
ATT_BLOCK = 128
N_SGU_GROUPS = 8
SGU_WIDTH = 1024
SGU_GROUP_DIM = SGU_WIDTH // N_SGU_GROUPS
SGU_CHUNK = 128
N_BRANCHES = 2
BRANCH_WIDTH = 1024
IN_COLS = 3 * ATT_WIDTH + 2 * SGU_WIDTH + N_BRANCHES * D_MODEL
N_REL_BUCKETS = 32
REL_MAX_DISTANCE = 2048
N_EXPERTS = 16
N_EXPERT_GROUPS = 4
EXPERTS_PER_GROUP = N_EXPERTS // N_EXPERT_GROUPS
TOP_K = 2
D_EXPERT = 1024
DEEPNORM_ALPHA = (2 * DEPTH) ** 0.25
DEEPNORM_BETA = (8 * DEPTH) ** -0.25
LN_EPS = 1e-5
N_MOD = 6

kernel_name = "hybrid_dilated_sgu_grouped_moe_deepnorm"

def layer_norm(x, g, b):
    xf = x.astype(jnp.float32)
    mu = xf.mean(-1, keepdims=True)
    var = jnp.mean(jnp.square(xf - mu), -1, keepdims=True)
    return ((xf - mu) * lax.rsqrt(var + LN_EPS)).astype(x.dtype) * g + b

def t5_causal_bucket(dist):
    max_exact = N_REL_BUCKETS // 2
    d_f = jnp.maximum(dist, 1).astype(jnp.float32)
    large = max_exact + (jnp.log(d_f / max_exact) / math.log(REL_MAX_DISTANCE / max_exact)
                         * (N_REL_BUCKETS - max_exact)).astype(jnp.int32)
    large = jnp.minimum(large, N_REL_BUCKETS - 1)
    return jnp.where(dist < max_exact, dist, large)

def dilated_window_attention(q, k, v, rel_bias, window, dilation):
    B, S, H, E = q.shape
    L = S // dilation
    span = window // dilation
    nb = -(-L // ATT_BLOCK)
    Lp = nb * ATT_BLOCK

    def to_classes(t):
        t = t.reshape(B, L, dilation, H, E).transpose(0, 2, 1, 3, 4)
        return jnp.pad(t, ((0, 0), (0, 0), (0, Lp - L), (0, 0), (0, 0)))

    qc, kc, vc = to_classes(q), to_classes(k), to_classes(v)
    qb = qc.reshape(B, dilation, nb, ATT_BLOCK, H, E)

    def windows(t):
        tp = jnp.pad(t, ((0, 0), (0, 0), (ATT_BLOCK, 0), (0, 0), (0, 0)))
        tp = tp.reshape(B, dilation, nb + 1, ATT_BLOCK, H, E)
        return jnp.concatenate([tp[:, :, :-1], tp[:, :, 1:]], axis=3)

    kw, vw = windows(kc), windows(vc)
    q_loc = jnp.arange(ATT_BLOCK)[:, None]
    k_loc = jnp.arange(2 * ATT_BLOCK)[None, :]
    delta = q_loc + ATT_BLOCK - k_loc
    band = (delta >= 0) & (delta <= span)
    bucket = t5_causal_bucket(jnp.maximum(delta, 0) * dilation)
    bias = jnp.transpose(rel_bias[bucket], (2, 0, 1)).astype(jnp.float32)
    k_abs = (jnp.arange(nb)[:, None] - 1) * ATT_BLOCK + k_loc
    mask = band[None] & (k_abs >= 0)[:, None, :]

    s = jnp.einsum('brnqhe,brnkhe->brnhqk', qb, kw).astype(jnp.float32) * (E ** -0.5) + bias
    s = jnp.where(mask[:, None], s, -jnp.inf)
    m = s.max(-1, keepdims=True)
    p = jnp.exp(s - m)
    denom = p.sum(-1, keepdims=True)
    o = jnp.einsum('brnhqk,brnkhe->brnqhe', (p / denom).astype(v.dtype), vw)
    lse = (m + jnp.log(denom))[..., 0]

    o = o.reshape(B, dilation, Lp, H, E)[:, :, :L].transpose(0, 2, 1, 3, 4).reshape(B, S, H, E)
    lse = lse.transpose(0, 1, 2, 4, 3).reshape(B, dilation, Lp, H)[:, :, :L]
    lse = lse.transpose(0, 2, 1, 3).reshape(B, S, H)
    return o, lse

def dilated_mixture(q, k, v, rel_bias):
    outs, lses = [], []
    for window, dilation in DILATED_PATTERNS:
        o, lse = dilated_window_attention(q, k, v, rel_bias, window, dilation)
        outs.append(o)
        lses.append(lse)
    wts = jax.nn.softmax(jnp.stack(lses, 0), axis=0)
    o = jnp.einsum('pbsh,pbshe->bshe', wts, jnp.stack(outs, 0).astype(jnp.float32))
    return o.astype(q.dtype)

def spatial_gating(z, ln_g, ln_b, w_s, b_s):
    B, S, _ = z.shape
    z = jax.nn.gelu(z)
    u, v = jnp.split(z, 2, axis=-1)
    nc = S // SGU_CHUNK
    v = v.reshape(B, nc, SGU_CHUNK, N_SGU_GROUPS, SGU_GROUP_DIM)
    v = layer_norm(v, ln_g.reshape(N_SGU_GROUPS, SGU_GROUP_DIM), ln_b.reshape(N_SGU_GROUPS, SGU_GROUP_DIM))
    causal = jnp.tril(jnp.ones((SGU_CHUNK, SGU_CHUNK), dtype=bool))
    w = jnp.where(causal[None], w_s, 0).astype(v.dtype)
    mixed = jnp.einsum('gts,bnsge->bntge', w, v) + b_s.T[:, :, None]
    return u * mixed.reshape(B, S, SGU_WIDTH)

def grouped_moe(h, router_w, router_b, w_gate, w_up, w_down):
    B, S, D = h.shape
    t = h.reshape(-1, D)
    logits = (t @ router_w).astype(jnp.float32) + router_b
    aff = jax.nn.softmax(logits, axis=-1)
    aff_g = aff.reshape(-1, N_EXPERT_GROUPS, EXPERTS_PER_GROUP)
    group_score = lax.top_k(aff_g, TOP_K)[0].sum(-1)
    best_group = jnp.argmax(group_score, axis=-1)
    in_group = jax.nn.one_hot(best_group, N_EXPERT_GROUPS, dtype=jnp.bool_)[:, :, None]
    masked = jnp.where(in_group, aff_g, -1.0).reshape(-1, N_EXPERTS)
    top_val, top_idx = lax.top_k(masked, TOP_K)
    top_w = top_val / top_val.sum(-1, keepdims=True)
    combine = jnp.sum(jax.nn.one_hot(top_idx, N_EXPERTS, dtype=jnp.float32) * top_w[..., None], axis=1)
    combine = combine.astype(t.dtype)
    y = jnp.zeros_like(t)
    for e in range(N_EXPERTS):
        hid = jax.nn.silu(t @ w_gate[e]) * (t @ w_up[e])
        y = y + combine[:, e:e + 1] * (hid @ w_down[e])
    return y.reshape(B, S, D)

def setup_inputs(seed: int = 0) -> dict:
    key = jax.random.key(seed)
    ks = jax.random.split(key, 24)
    nrm = lambda k, shape, s: jax.random.normal(k, shape, jnp.float32) * s
    D, L = D_MODEL, DEPTH
    return {
        'x': nrm(ks[0], (BATCH, SEQ, D), 1.0),
        'c': nrm(ks[1], (BATCH, D), 1.0),
        'rel_bias': nrm(ks[2], (N_REL_BUCKETS, N_ATT_HEADS), 0.5),
        'router_w': nrm(ks[3], (D, N_EXPERTS), D ** -0.5),
        'router_b': nrm(ks[4], (N_EXPERTS,), 0.01),
        'ada_w': nrm(ks[5], (L, D, N_MOD * D), D ** -0.5),
        'ada_b': nrm(ks[6], (L, N_MOD * D), 0.02),
        'w_in': nrm(ks[7], (L, D, IN_COLS), D ** -0.5),
        'sgu_ln_g': 1.0 + nrm(ks[8], (L, SGU_WIDTH), 0.02),
        'sgu_ln_b': nrm(ks[9], (L, SGU_WIDTH), 0.02),
        'sgu_w': nrm(ks[10], (L, N_SGU_GROUPS, SGU_CHUNK, SGU_CHUNK), SGU_CHUNK ** -0.5),
        'sgu_b': 1.0 + nrm(ks[11], (L, N_SGU_GROUPS, SGU_CHUNK), 0.02),
        'w_branch': nrm(ks[12], (L, N_BRANCHES, BRANCH_WIDTH, D), BRANCH_WIDTH ** -0.5),
        'w_out': nrm(ks[13], (L, D, D), DEEPNORM_BETA * D ** -0.5),
        'ln1_g': 1.0 + nrm(ks[14], (L, D), 0.02),
        'ln1_b': nrm(ks[15], (L, D), 0.02),
        'ln2_g': 1.0 + nrm(ks[16], (L, D), 0.02),
        'ln2_b': nrm(ks[17], (L, D), 0.02),
        'exp_w_gate': nrm(ks[18], (L, N_EXPERTS, D, D_EXPERT), D ** -0.5),
        'exp_w_up': nrm(ks[19], (L, N_EXPERTS, D, D_EXPERT), D ** -0.5),
        'exp_w_down': nrm(ks[20], (L, N_EXPERTS, D_EXPERT, D), DEEPNORM_BETA * D_EXPERT ** -0.5),
    }

def reference(x, c, rel_bias, router_w, router_b, ada_w, ada_b, w_in, sgu_ln_g, sgu_ln_b,
              sgu_w, sgu_b, w_branch, w_out, ln1_g, ln1_b, ln2_g, ln2_b,
              exp_w_gate, exp_w_up, exp_w_down):
    B, S, D = x.shape
    cond = jax.nn.silu(c)
    for l in range(DEPTH):
        mod = cond @ ada_w[l] + ada_b[l]
        sh1, sc1, g1, sh2, sc2, g2 = jnp.split(mod[:, None, :], N_MOD, axis=-1)

        xm = x * (1 + sc1) + sh1
        proj = xm @ w_in[l]
        q, k, v, z, gate_logits = jnp.split(
            proj, [ATT_WIDTH, 2 * ATT_WIDTH, 3 * ATT_WIDTH, 3 * ATT_WIDTH + 2 * SGU_WIDTH], axis=-1)
        hs = (B, S, N_ATT_HEADS, HEAD_DIM)
        y_att = dilated_mixture(q.reshape(hs), k.reshape(hs), v.reshape(hs), rel_bias)
        y_att = y_att.reshape(B, S, ATT_WIDTH)
        y_sgu = spatial_gating(z, sgu_ln_g[l], sgu_ln_b[l], sgu_w[l], sgu_b[l])
        branches = jnp.einsum('bspw,pwd->bspd', jnp.stack([y_att, y_sgu], axis=2), w_branch[l])
        gates = jax.nn.sigmoid(gate_logits.reshape(B, S, N_BRANCHES, D))
        mix = jnp.sum(gates * branches, axis=2) @ w_out[l]
        x = layer_norm(DEEPNORM_ALPHA * x + g1 * mix, ln1_g[l], ln1_b[l])

        hm = x * (1 + sc2) + sh2
        f = grouped_moe(hm, router_w, router_b, exp_w_gate[l], exp_w_up[l], exp_w_down[l])
        x = layer_norm(DEEPNORM_ALPHA * x + g2 * f, ln2_g[l], ln2_b[l])
    return x


_drawn_inputs = setup_inputs


def setup_inputs(seed=0):
    import zlib

    import numpy as np

    out = dict(_drawn_inputs(seed))
    spreads = {}
    factors = {'router_b': 8.0,
     'sgu_ln_g': 3.626,
     'sgu_ln_b': 8.0,
     'sgu_b': 3.578,
     'ln2_g': 2.903,
     'ln2_b': 2.827}
    for name, (base, spread) in spreads.items():
        noise = np.random.default_rng([zlib.crc32(name.encode()), seed]).standard_normal(out[name].shape)
        drawn = base * np.exp(spread * noise) if base else spread * noise
        out[name] = __import__('jax').numpy.asarray(drawn.astype(out[name].dtype))
    for name, factor in factors.items():
        out[name] = (out[name] * factor).astype(out[name].dtype)
    return out
```

```python
from contextlib import ExitStack

import concourse.bass as bass
from concourse import mybir

F32 = mybir.dt.float32
I32 = mybir.dt.int32
ALU = mybir.AluOpType
ACT = mybir.ActivationFunctionType
AX_X = mybir.AxisListType.X

P = 128
D = 2048
T = 256
TT = T // P
KC = D // P
H = 8
G = 8
MOD = 6
NE = 16
NG = 4
F = 1024
PATTERNS = ((128, 1), (512, 4), (2048, 16))
BUCKETS = 32
ALPHA = 2.0 ** 0.25
EPS = 1e-5
QSCALE = float(P) ** -0.5
UW = 512
RING = 3
SLOT = KC * UW
CAP = 64
XT = T // CAP
GRP = 4
TOE = 384
FAR = 1024.0

W_UNITS = ([("q", 0), ("q", 1), ("k", 0), ("k", 1), ("v", 0), ("v", 1), ("u", 0), ("u", 1), ("z", 0), ("z", 1)]
           + [(kind, j) for j in range(4) for kind in ("gate0", "gate1", "branch")]
           + [("out", j) for j in range(4)])
IN_COL = {"q": 0, "k": 1024, "v": 2048, "u": 3072, "z": 4096, "gate0": 5120, "gate1": 7168}
SH1, SC1, G1, SH2, SC2, G2 = range(MOD)
ADA_UNITS = [(m, j) for j in range(4) for m in (SC1, SH1)] + [(m, j) for m in (G1, SC2, SH2, G2) for j in range(4)]
ADA_FIRST = 8
STREAM = [("ada", a) for a in range(ADA_FIRST)]
for _i in range(len(W_UNITS)):
    STREAM.append(("w", _i))
    if ADA_FIRST + _i < len(ADA_UNITS):
        STREAM.append(("ada", ADA_FIRST + _i))
AT = {u: n for n, u in enumerate(STREAM)}
NFRONT = len(STREAM)
NW = len(W_UNITS)
E_UNITS = 6
JOBS = [(i, m) for i, (kind, _) in enumerate(W_UNITS) for m in range(4 if kind == "branch" else 2)]
JOB = {im: n for n, im in enumerate(JOBS)}


def by_dve(n):
    return W_UNITS[JOBS[n][0]][0] in ("branch", "out")


def evictions(n):
    return sum(by_dve(k) == by_dve(n) for k in range(n + 1))


SCHEDULE = []
ADA_ROWS = {(1, 0): range(0, 6), (1, 1): range(6, 12), (0, 0): range(12, KC)}
_att = 0
for _i, (_kind, _j) in enumerate(W_UNITS):
    for _m in range(4 if _kind == "branch" else 2):
        for _h in range(2):
            SCHEDULE.append(("part", _i, _m, _h))
            _a = ADA_FIRST + _i - (_m == 0)
            if (_m, _h) in ADA_ROWS and ADA_FIRST <= _a < len(ADA_UNITS):
                SCHEDULE.append(("adapart", _a, ADA_ROWS[_m, _h]))
            if _i >= 6 and _att < H + 2:
                SCHEDULE.append(("att", _att))
                _att += 1
    if 1 <= _i <= len(ADA_UNITS) - ADA_FIRST:
        SCHEDULE.append(("ada", ADA_FIRST + _i - 1))
    if _i == 9:
        SCHEDULE.append(("norm",))
    if _i == 11:
        SCHEDULE += [("mix", m) for m in range(4)]

X_PE, X_ACT, X_DVE = 17, 7, 13
PE_SEC = {"A": 3, "B": 1, "C": 1, "D": 1, "E": 2, "F": 9}
ACT_SEC = {"A": 3, "B": 1, "C": 1, "D": 1, "E": 1, "F": 0}
DVE_SEC = {"A": 1, "B": 1, "C": 0, "D": 1, "E": 0, "F": 10}
BANK_JOBS = 4 + 4 * GRP


def program(nc, x_tok_d, x_T_d, c_T_d, rel_bias_d, router_w_d, router_b_d, ada_w_d, ada_b_d, w_in_d,
            sgu_g_d, sgu_b_d, sgu_wT_d, sgu_bias_d, w_branch_d, w_out_d, ln1_g_d, ln1_b_d, ln2_g_d, ln2_b_d,
            w_gate_d, w_up_d, w_down_d, square_d, slots_d, buckets_d, out_d):
    with ExitStack() as ctx:
        def sb(name, cols, dt=F32, parts=P):
            return ctx.enter_context(nc.sbuf_tensor(name, [parts, cols], dt))

        def sem(name):
            return ctx.enter_context(nc.semaphore(name))

        ring = sb("ring", RING * SLOT)
        region_a = sb("region_a", KC * T)
        region_b = sb("region_b", KC * T)
        region_c = sb("region_c", 2048)
        region_d = sb("region_d", 2048)
        region_e = sb("region_e", 2048)
        region_f = sb("region_f", 2048)
        region_x = sb("region_x", TT * D)
        g1b = sb("g1b", D)
        g2x = sb("g2x", 2 * UW)
        sgu_wT = sb("sgu_wT", G * P)
        work = sb("work", 1024)
        work2 = sb("work2", 1024)
        square = sb("square", 2 * P)
        slots = sb("slots", XT * 2 * CAP)
        ones = sb("ones", P)
        eps = sb("eps", 1)
        condT = sb("condT", KC)
        cT = sb("cT", KC)
        ada_bias = sb("ada_bias", UW)
        sgu_bias = sb("sgu_bias", P, parts=G)
        small = sb("small", 640)
        modcol = sb("modcol", 4 * KC)
        router_w = sb("router_w", KC * NE)
        counts = sb("counts", NE, I32)

        psum = [ctx.enter_context(nc.psum_tensor(f"bank{i}", [P, 512], F32)) for i in range(8)]

        def slot(n):
            return ring[:, (n % RING) * SLOT:(n % RING + 1) * SLOT]

        ident = square[:, 0:P]
        upper = square[:, P:2 * P]
        xmT = region_a[:, :].rearrange("p (k t) -> p k t", t=T)
        acc = region_a[:, :].rearrange("p (a d) -> p a d", a=TT)
        qT = region_b[:, 0:H * T].rearrange("p (h t) -> p h t", t=T)
        kT = region_b[:, H * T:2 * H * T].rearrange("p (h t) -> p h t", t=T)
        mixT = region_b[:, :].rearrange("p (k t) -> p k t", t=T)
        hmT = mixT
        xe = mixT
        v = region_c[:, :].rearrange("p (a n) -> p a n", a=TT)
        gates = region_c[:, :].rearrange("p (c b t) -> p c b t", c=4, b=2)
        uT = region_d[:, :].rearrange("p (g t) -> p g t", t=T)
        zv = region_e[:, :].rearrange("p (a n) -> p a n", a=TT)
        attT = region_f[:, :].rearrange("p (h t) -> p h t", t=T)
        toep = region_x[:, 0:H * T].rearrange("p (h s) -> p h s", s=T)
        sgu_g = region_x[:, 2048:3072]
        sgu_b = region_x[:, 3072:4096]
        x1 = region_x[:, :].rearrange("p (a d) -> p a d", a=TT)
        ln1g, ln1b = region_e[:, :], region_d[:, :]
        ln2g = slot(NFRONT + NE * E_UNITS - 3)[:, 0:D]
        ln2b = slot(NFRONT + NE * E_UNITS - 3)[:, D:2 * D]
        xx = [(region_c if r == 1 else region_c if r == 2 else region_d)[:, (0, 1024, 0)[r - 1]:(0, 1024, 0)[r - 1] + 1024]
              .rearrange("p (k s) -> p k s", s=CAP) for r in range(1, XT)]
        hot = region_e[:, 0:TT * GRP * CAP].rearrange("p (a e s) -> p a e s", a=TT, e=GRP)
        hotx = region_e[:, 512:1024].rearrange("p (r a s) -> p r a s", r=XT, a=TT)
        hotw = region_e[:, 1024:1024 + TT * 2 * CAP].rearrange("p (a c s) -> p a c s", a=TT, c=2)
        hotwx = region_e[:, 1280:1280 + TT * 2 * CAP].rearrange("p (a c s) -> p a c s", a=TT, c=2)
        back = region_d[:, 1024:2048].rearrange("p (r a t) -> p r a t", r=XT, a=TT)
        hidT = region_f[:, :].rearrange("p (r k s) -> p r k s", r=XT, k=8)
        ysb = [sgu_wT[:, 0:512], sgu_wT[:, 512:1024]]
        ysbx = region_e[:, 1536:2048]
        silu_g = [work[:, 0:256], work[:, 256:512]]
        hid = [work2[:, 0:256], work2[:, 256:512]]
        hidx = [None, work[:, 512:768], work[:, 768:1024], work2[:, 512:768]]
        tmp = [work[:, 0:512], work[:, 512:1024]]
        prob = [work2[:, 0:384], work2[:, 384:768]]
        pT = sb("pT", 2 * 3 * P)
        pTs = [pT[:, 0:3 * P], pT[:, 3 * P:]]
        ada_rows = sb("ada_rows", 2 * UW)
        ada_row = [ada_rows[:, 0:UW], ada_rows[:, UW:]]
        att_o = small[:, 0:16]
        nmax2 = [att_o[:, 0:2], att_o[:, 2:4]]
        rsum2 = [att_o[:, 4:6], att_o[:, 6:8]]
        rinv = att_o[:, 8:10]
        zstat = small[:, 16:16 + 2 * G * 6].rearrange("p (n s) -> p n s", s=6)
        zmv = small[:, 112:112 + 2 * G * 2].rearrange("p (n s) -> p n s", s=2)
        zrstd = small[:, 144:160]
        lstat = small[:, 160:160 + TT * 24].rearrange("p (a n s) -> p a n s", a=TT, s=6)
        lmv = small[:, 208:212].rearrange("p (a s) -> p a s", s=2)
        lrstd = small[:, 212:214]
        router_b = small[:, 216:232]
        lgT = work[0:NE, 0:T]
        aff = small[:, 232:264]
        wts = small[:, 264:296]
        place = small[:, 296:328]
        mask = small[:, 328:360]
        rank = small[:, 360:392]
        sel = small[:, 392:424]
        best = small[:, 424:456]
        gsc = small[:, 456:464]
        grank = small[:, 464:472]
        cmp_ = small[:, 480:608]
        gcmp = small[:, 608:640]
        toe_row = region_f[0:H, 0:TOE]
        buckets = region_f[0:BUCKETS + 1, TOE:2 * TOE]
        rel = sb("rel", H, parts=BUCKETS + 1)
        toe_dram = nc.dram_tensor("toe_dram", (H, P, TOE), F32, kind="Internal")

        loaded = [sem(f"ring_loaded{i}") for i in range(RING)]
        slot_freed = sem("slot_seen_free_by_sp")
        extra_end = {e: sem(f"extra_section_end_{e}") for e in ("act", "dve")}
        used_ac = sem("first_unit_of_pair_used")
        s_c = sem("c_loaded")
        s_xT = sem("xT_loaded")
        s_const = sem("const_loaded")
        s_rel = sem("rel_loaded")
        s_sguw = sem("sguw_loaded")
        s_sgubc = sem("sgu_norm_loaded")
        s_router = sem("router_loaded")
        s_x = sem("x_loaded")
        s_ln1 = sem("ln1_loaded")
        s_ln2 = sem("ln2_loaded")
        s_toed = sem("toeplitz_stored")
        s_toe = sem("toeplitz_loaded")
        s_out = sem("out_stored")
        s_ones = sem("ones_set")
        s_relone = sem("rel_one_set")
        s_toep = sem("toeplitz_row_summed")
        s_toer = sem("toeplitz_row_ready")
        s_cond = sem("cond_ready")
        ada_acc = sem("ada_acc_ready")
        ada_sum = sem("ada_summed")
        ada_out = sem("ada_taken_dve")
        ada_outa = sem("ada_taken_act")
        s_sc2 = sem("scale2_ready")
        xm_ready = sem("xm_ready")
        causal = sem("gating_causal")
        link_dve = sem("dve_link")
        job_full = sem("job_full")
        act_emptied = sem("job_emptied_act")
        dve_emptied = sem("job_emptied_dve")
        sc_full = sem("scores_full")
        sc_taken = sem("scores_taken")
        s_max = sem("row_max_ready")
        s_exp = sem("exp_ready")
        p_norm = sem("probs_ready")
        pt_full = sem("probsT_full")
        pt_taken = sem("probsT_taken")
        o_full = sem("att_full")
        o_taken = sem("att_taken")
        z_var = sem("gating_var_ready")
        z_std = sem("gating_std_ready")
        z_ready = sem("gating_v_ready")
        mix_full = sem("mixed_full")
        mix_taken = sem("mixed_taken")
        mix_ready = sem("mixT_ready")
        l_var = sem("ln_var_ready")
        l_std = sem("ln_std_ready")
        x1_ready = sem("x1_ready")
        acc_ready = sem("acc_ready")
        xt_full = sem("x1T_full")
        xt_taken = sem("x1T_taken")
        lg_full = sem("logitsT_full")
        lg_copied = sem("logitsT_copied")
        lg_turned = sem("logits_turned")
        lg_sub = sem("logits_shifted")
        lg_exp = sem("logits_exp")
        mask_ready = sem("mask_ready")
        place_full = sem("place_full")
        routed = sem("routed")
        hot_ready = sem("hot_ready")
        hotw_ready = sem("hotw_ready")
        t_full = sem("turned_full")
        t_taken = sem("turned_taken")
        m_full = [sem("bank6_full"), sem("bank7_full")]
        m_taken = [sem("bank6_taken"), sem("bank7_taken")]
        h_full = sem("h_full")
        h_silu = sem("h_silu")
        hid_ready = sem("hid_ready")
        y_full = sem("y_full")
        y_ready = sem("y_ready")
        x_pe = [None] + [sem(f"extra{r}_pe") for r in range(1, XT)]
        x_act = [None] + [sem(f"extra{r}_act") for r in range(1, XT)]
        x_dve = [None] + [sem(f"extra{r}_dve") for r in range(1, XT)]
        out_ready = sem("out_ready")

        block = ctx.enter_context(nc.Block())

        def unit_loaded(eng, n):
            eng.wait_ge(loaded[n % RING], 32 * (n // RING + 1))

        def e_unit_loaded(eng, g, t):
            n = NFRONT + t
            eng.wait_ge(loaded[n % RING], g * (32 * GRP * E_UNITS // RING) + 32 * (n // RING + 1))

        def unit_used(eng, n):
            kind, i = STREAM[n]
            if kind == "w":
                eng.wait_ge(job_full, JOB[i, 3 if W_UNITS[i][0] == "branch" else 1] + 1)
            else:
                eng.wait_ge(ada_acc, i + 1)

        @block.sync
        def _(sp):
            for n, (kind, i) in enumerate(STREAM):
                if n >= RING:
                    unit_used(sp, n - RING)
                if kind == "ada":
                    m, j = ADA_UNITS[i]
                    src, col = ada_w_d, m * D + j * UW
                elif W_UNITS[i][0] == "branch":
                    src, col = w_branch_d, W_UNITS[i][1] * UW
                elif W_UNITS[i][0] == "out":
                    src, col = w_out_d, W_UNITS[i][1] * UW
                else:
                    src, col = w_in_d, IN_COL[W_UNITS[i][0]] + W_UNITS[i][1] * UW
                dst = slot(n).rearrange("p (k n) -> p k n", n=UW)
                for h in range(2):
                    rows = src[h * 1024:(h + 1) * 1024, col:col + UW].rearrange("(k p) n -> p k n", p=P)
                    sp.dma_start(dst[:, 8 * h:8 * h + 8, :], rows).then_inc(loaded[n % RING], 16)

            def load_unit(g, t):
                e, s = g * GRP + t // E_UNITS, t % E_UNITS
                n = NFRONT + t
                for h in range(2):
                    if s < 4:
                        j, half = s // 2, s % 2
                        dst = slot(n).rearrange("p (k u n) -> p k u n", k=8, u=2)[:, :, h, :]
                        src = (w_gate_d, w_up_d)[h][bass.ds(e, 1), half * 1024:(half + 1) * 1024, j * 512:(j + 1) * 512]
                    else:
                        q = s - 4
                        dst = slot(n).rearrange("p (k n) -> p k n", k=8)[:, 4 * h:4 * h + 4, :]
                        src = w_down_d[bass.ds(e, 1), h * 512:(h + 1) * 512, q * 1024:(q + 1) * 1024]
                    sp.dma_start(dst, src.rearrange("o (k p) n -> p (o k) n", p=P)).then_inc(loaded[n % RING], 16)

            def unit_multiplied(g, t):
                ne, s = g * GRP + t // E_UNITS, t % E_UNITS
                done = (used_ac, h_full, used_ac, h_full, y_full, y_full)[s]
                sp.wait_ge(done, ne * 2 + (1, 1, 2, 2, 1, 2)[s])
                sp.sem_inc(slot_freed, 1)

            for t in range(RING):
                unit_used(sp, NFRONT + t - RING)
                load_unit(0, t)
            units = GRP * E_UNITS
            with sp.Fori(0, NE // GRP - 1) as g:
                for t in range(units):
                    unit_multiplied(g, t)
                    load_unit(g, t + RING)
            for t in range(units - RING):
                unit_multiplied(NE // GRP - 1, t)
                load_unit(NE // GRP - 1, t + RING)
            unit_multiplied(NE // GRP - 1, units - RING)
            sp.dma_start(ln2g, ln2_g_d.to_broadcast([P, D])).then_inc(s_ln2, 16)
            sp.dma_start(ln2b, ln2_b_d.to_broadcast([P, D])).then_inc(s_ln2, 16)
            for a in range(TT):
                sp.wait_ge(out_ready, a + 1)
                sp.dma_start(out_d[a * P:(a + 1) * P, :], acc[:, a, :]).then_inc(s_out, 16)
            sp.wait_ge(s_out, 16 * TT)

        @block.gpsimd
        def _(pool):
            pool.memset(eps[:, :], EPS).then_inc(s_ones, 1)
            pool.memset(ones[:, :], 1.0).then_inc(s_ones, 1)
            pool.wait_ge(s_sguw, 16)
            w3 = sgu_wT[:, :].rearrange("p (g t) -> p g t", g=G)
            pool.affine_select(out=w3, in_=w3, compare_op=ALU.is_ge, fill=0.0, base=0,
                               pattern=[[0, G], [1, P]], channel_multiplier=-1).then_inc(causal, 1)

        def tokens(r, k, le):
            return xe[:, k, le * CAP:(le + 1) * CAP] if r == 0 else xx[r - 1][:, k, :]

        def expert_pe(pe, mm, g, le, count):
            ne = g * GRP + le

            def gate_up(r, j, half):
                bank = psum[j] if r == 0 else psum[1 + r]
                w = slot(NFRONT + le * E_UNITS + 2 * j + half).rearrange("p (k u n) -> p k u n", k=8, u=2)
                for k in range(8):
                    for c in range(2):
                        last = nc.tensor.matmul(bank[64 * c:64 * c + 64, :], tokens(r, 8 * half + k, le),
                                                w[:, k, :, 256 * c:256 * c + 256],
                                                start=(half == 0 and k == 0), stop=(half == 1 and k == 7),
                                                tile_position=(0, 64 * c), skip_group_check=True)
                return last

            def down(r, q, ks):
                bank = psum[q] if r == 0 else psum[1 + r]
                w = slot(NFRONT + le * E_UNITS + 4 + q).rearrange("p (k n) -> p k n", k=8)
                for k in ks:
                    for c in range(2):
                        last = nc.tensor.matmul(bank[64 * c:64 * c + 64, :], hidT[:, r, k, :],
                                                w[:, k, 512 * c:512 * c + 512],
                                                start=(k == 0), stop=(k == 7),
                                                tile_position=(0, 64 * c), skip_group_check=True)
                return last

            def turn(src):
                for b in range(2):
                    last = nc.tensor.transpose(psum[5][:, b * P:(b + 1) * P], src[:, b * P:(b + 1) * P], ident)
                return last

            def scatter(bank, r, y, c, a):
                return nc.tensor.matmul(bank[:, :], back[64 * c:64 * c + 64, r, a, :], y[64 * c:64 * c + 64, :],
                                        start=True, stop=True, tile_position=(64 * c, 0))

            def extra(r, sec):
                xp, xa, xd = x_pe[r], x_act[r], x_dve[r]
                bp, ba, bd = ne * X_PE, ne * X_ACT, ne * X_DVE
                if sec == "A":
                    pe.wait_ge(xd, bd + 1)
                    for half in range(2):
                        if half == 1:
                            pe.wait_ge(xa, ba + 1)
                        for k in range(8):
                            for a in range(TT):
                                last = mm(psum[1 + r][:, k * CAP:(k + 1) * CAP],
                                          x1[:, a, (8 * half + k) * P:(8 * half + k + 1) * P], hotx[:, r, a, :],
                                          a == 0, a == TT - 1)
                        last.then_inc(xp, 1)
                    pe.wait_ge(t_taken, ne * 3 + 1)
                    turn(hotwx.rearrange("p a c s -> p (a c s)")).then_inc(xp, 1)
                    pe.wait_ge(xa, ba + 3)
                    gate_up(r, 0, 0)
                    pe.wait_ge(xp, bp + 3)
                elif sec == "B":
                    gate_up(r, 0, 1).then_inc(xp, 1)
                    pe.wait_ge(xp, bp + 4)
                elif sec == "C":
                    pe.wait_ge(xd, bd + 2)
                    gate_up(r, 1, 0)
                    pe.wait_ge(t_taken, ne * 3 + 2)
                    turn(hidx[r]).then_inc(xp, 1)
                    pe.wait_ge(xa, ba + 5)
                elif sec == "D":
                    gate_up(r, 1, 1).then_inc(xp, 1)
                    pe.wait_ge(xd, bd + 3)
                elif sec == "E":
                    pe.wait_ge(t_taken, ne * 3 + 3)
                    turn(hidx[r]).then_inc(xp, 1)
                    pe.wait_ge(xa, ba + 7)
                    down(r, 0, range(8)).then_inc(xp, 1)
                    pe.wait_ge(xp, bp + 8)
                else:
                    for b in range(2):
                        pe.wait_ge(m_taken[b], g * BANK_JOBS + 4 * (le + 1) + 1)
                    pe.wait_ge(xd, bd + 4)
                    for q in range(2):
                        if q == 1:
                            pe.wait_ge(xd, bd + 8)
                            down(r, 1, range(8)).then_inc(xp, 1)
                            pe.wait_ge(xd, bd + 9)
                        for a in range(TT):
                            for c in range(2):
                                n = q * 4 + a * 2 + c
                                if a == 1:
                                    pe.wait_ge(xd, bd + 5 + q * 5 + c)
                                scatter(psum[6 + c], r, ysbx, c, a).then_inc(xp, 1)
                    pe.wait_ge(xd, bd + 13)

            def extras(sec):
                for least, rs in ((CAP, (1,)), (2 * CAP, (2, 3))):
                    with pe.If(count > least):
                        for r in rs:
                            extra(r, sec)
                    with pe.Else():
                        for r in rs:
                            pe.sem_inc(x_pe[r], PE_SEC[sec])

            t = le * E_UNITS
            if le == 0:
                for b in range(2):
                    pe.wait_ge(m_taken[b], g * BANK_JOBS + 5)
            pe.wait_ge(hotw_ready, ne + 1)
            pe.wait_ge(t_taken, ne * 3 + 1)
            turn(hotw.rearrange("p a c s -> p (a c s)")).then_inc(t_full, 1)
            pe.wait_ge(t_taken, ne * 3 + 2)
            e_unit_loaded(pe, g, t)
            extras("A")
            pe.wait_ge(y_ready, ne * 2 + 1)
            gate_up(0, 0, 0).then_inc(used_ac, 1)
            e_unit_loaded(pe, g, t + 1)
            extras("B")
            gate_up(0, 0, 1).then_inc(h_full, 1)
            e_unit_loaded(pe, g, t + 2)
            extras("C")
            pe.wait_ge(y_ready, ne * 2 + 2)
            gate_up(0, 1, 0).then_inc(used_ac, 1)
            pe.wait_ge(hid_ready, ne * 2 + 1)
            turn(hid[0]).then_inc(t_full, 1)
            e_unit_loaded(pe, g, t + 3)
            extras("D")
            gate_up(0, 1, 1).then_inc(h_full, 1)
            e_unit_loaded(pe, g, t + 4)
            extras("E")
            pe.wait_ge(t_taken, ne * 3 + 3)
            down(0, 0, range(4))
            pe.wait_ge(hid_ready, ne * 2 + 2)
            turn(hid[1]).then_inc(t_full, 1)
            pe.wait_ge(t_taken, ne * 3 + 4)
            down(0, 0, range(4, 8)).then_inc(y_full, 1)
            e_unit_loaded(pe, g, t + 5)
            extras("F")
            down(0, 1, range(8)).then_inc(y_full, 1)
            for q in range(2):
                pe.wait_ge(y_ready, ne * 2 + 3 + q)
                for a in range(TT):
                    for c in range(2):
                        pe.wait_ge(m_taken[c], g * BANK_JOBS + 4 * (le + 1) + 1 + 2 * q + a)
                        scatter(psum[6 + c], 0, ysb[q], c, a).then_inc(m_full[c], 1)

        @block.tensor
        def _(pe):
            def mm(out, lhsT, rhs, start, stop):
                return nc.tensor.matmul(out, lhsT, rhs, start=start, stop=stop)

            pe.wait_ge(s_ones, 2)
            pe.wait_ge(s_const, 32)
            pe.wait_ge(s_rel, 32)
            pe.wait_ge(s_relone, 1)
            mm(psum[4][0:H, 0:TOE], rel[:, :], buckets, True, True).then_inc(s_toep, 1)

            def ada_step(a):
                m, j = ADA_UNITS[a]
                b = a - ADA_FIRST
                src = ada_row[a % 2]
                pe.wait_ge(ada_acc, a + 1)
                if 1 <= a <= ADA_FIRST:
                    pe.wait_ge(ada_out, a)
                elif a > ADA_FIRST:
                    pe.wait_ge(ada_outa, b)
                pick = ident[0:MOD * 4, 4 * m + j:4 * m + j + 1]
                if m in (G1, G2):
                    mm(psum[7][:, :], ones[:, :], src, True, False)
                    last = mm(psum[7][:, :], pick.to_broadcast([MOD * 4, P]), ada_bias[0:MOD * 4, :], False, True)
                else:
                    for c in range(4):
                        cols = slice(c * P, (c + 1) * P)
                        mm(psum[7][:, c:c + 1], src[:, cols], ones[:, 0:1], True, False)
                        last = mm(psum[7][:, c:c + 1], ada_bias[0:MOD * 4, cols], pick, False, True)
                last.then_inc(ada_sum, 1)

            for a in range(ADA_FIRST):
                ada_step(a)

            def part(i, m, h):
                kind, j = W_UNITS[i]
                n, job = AT[("w", i)], JOB[i, m]
                bank = psum[job % 4]
                if m == 0 and h == 0:
                    unit_loaded(pe, n)
                    if i == 0:
                        pe.wait_ge(xm_ready, 4)
                    if i == W_UNITS.index(("branch", 0)):
                        pe.wait_ge(o_taken, H)
                        pe.wait_ge(mix_taken, 4)
                    if kind == "out" and j == 0:
                        pe.wait_ge(mix_ready, KC)
                if h == 0 and job >= 4:
                    pe.wait_ge(dve_emptied if by_dve(job - 4) else act_emptied, evictions(job - 4))
                w = slot(n).rearrange("p (k n) -> p k n", n=UW)
                if kind == "branch":
                    src = attT if h == 0 else uT
                    for k in range(8):
                        last = mm(bank[:, h * T:(h + 1) * T], w[:, 8 * h + k, m * P:(m + 1) * P], src[:, k, :],
                                  k == 0, k == 7)
                elif kind in ("v", "z", "out"):
                    src = mixT if kind == "out" else xmT
                    for k in range(8 * h, 8 * h + 8):
                        last = mm(bank[:, :], src[:, k, m * P:(m + 1) * P], w[:, k, :], k == 0, k == KC - 1)
                else:
                    c = 2 * m + h
                    for k in range(KC):
                        last = mm(bank[:, h * T:(h + 1) * T], w[:, k, c * P:(c + 1) * P], xmT[:, k, :],
                                  k == 0, k == KC - 1)
                if h == 1:
                    last.then_inc(job_full, 1)

            def att(s):
                if s < H:
                    if s == 0:
                        pe.wait_ge(act_emptied, 12)
                    else:
                        pe.wait_ge(sc_taken, s)
                    mm(psum[4][:, 0:P], qT[:, s, 0:P], kT[:, s, 0:P], True, True)
                    mm(psum[4][:, P:3 * P], qT[:, s, P:T], kT[:, s, :], True, True).then_inc(sc_full, 1)
                if 1 <= s <= H:
                    pe.wait_ge(p_norm, s)
                    if s >= 2:
                        pe.wait_ge(pt_taken, s - 1)
                    pr = prob[(s - 1) % 2]
                    for b in range(3):
                        last = nc.tensor.transpose(psum[5][:, b * P:(b + 1) * P], pr[:, b * P:(b + 1) * P], ident)
                    last.then_inc(pt_full, 1)
                if s >= 2:
                    h = s - 2
                    pe.wait_ge(pt_taken, h + 1)
                    if h >= 1:
                        pe.wait_ge(o_taken, h)
                    ptb = pTs[h % 2]
                    mm(psum[6][:, 0:T], v[:, 0, h * P:(h + 1) * P], ptb[:, 0:T], True, False)
                    mm(psum[6][:, P:T], v[:, 1, h * P:(h + 1) * P], ptb[:, T:3 * P], False, True).then_inc(o_full, 1)

            def mix(m):
                a = m // 2
                if m == 0:
                    pe.wait_ge(z_ready, 1)
                    pe.wait_ge(causal, 1)
                    pe.wait_ge(pt_taken, H)
                    pe.wait_ge(o_taken, H)
                    pe.wait_ge(sc_taken, H)
                if m == 3:
                    pe.wait_ge(mix_taken, 1)
                bank = psum[4 + m % 3]
                for q in range(4):
                    grp = 4 * (m % 2) + q
                    out = bank[:, q * P:(q + 1) * P]
                    mm(out, zv[:, a, grp * P:(grp + 1) * P], sgu_wT[:, grp * P:(grp + 1) * P], True, False)
                    last = mm(out, ident[0:G, grp:grp + 1].to_broadcast([G, P]), sgu_bias[:, :], False, True)
                last.then_inc(mix_full, 1)

            for step in SCHEDULE:
                if step[0] == "part":
                    part(*step[1:])
                elif step[0] == "att":
                    att(step[1])
                elif step[0] == "ada":
                    ada_step(step[1])
                elif step[0] == "mix":
                    mix(step[1])

            pe.wait_ge(x1_ready, TT)

            def logits(m):
                pe.wait_ge(xt_taken, m + 1)
                for k in (2 * m, 2 * m + 1):
                    last = mm(psum[5][0:NE, 0:T], router_w[:, k * NE:(k + 1) * NE], hmT[:, k, :], k == 0, k == KC - 1)
                if m == KC // 2 - 1:
                    last.then_inc(lg_full, 1)

            pe.wait_ge(s_router, 48)
            for m in range(KC // 2):
                if m >= 2:
                    pe.wait_ge(xt_taken, m - 1)
                for kk in range(2):
                    for a in range(TT):
                        last = nc.tensor.transpose(psum[6 + m % 2][:, kk * T + a * P:kk * T + (a + 1) * P],
                                                   x1[:, a, (2 * m + kk) * P:(2 * m + kk + 1) * P], ident)
                last.then_inc(xt_full, 1)
                if m >= 1:
                    logits(m - 1)
            logits(KC // 2 - 1)
            pe.wait_ge(lg_copied, 1)
            for a in range(TT):
                last = nc.tensor.transpose(psum[4][:, a * NE:(a + 1) * NE], lgT[:, a * P:(a + 1) * P], ident[0:NE, 0:NE])
            last.then_inc(lg_turned, 1)
            pe.wait_ge(mask_ready, 1)
            mm(psum[5][:, 0:NE], upper, mask[:, 0:NE], True, True)
            mm(psum[5][:, NE:2 * NE], ones[:, :], mask[:, 0:NE], True, False)
            mm(psum[5][:, NE:2 * NE], upper, mask[:, NE:2 * NE], False, True)
            mm(psum[5][:, 2 * NE:3 * NE], ones[:, :], mask[:, 0:NE], True, False)
            mm(psum[5][:, 2 * NE:3 * NE], ones[:, :], mask[:, NE:2 * NE], False, True).then_inc(place_full, 1)

            pe.wait_ge(routed, 1)
            with pe.Fori(0, NE // GRP) as g:
                pe.wait_ge(hot_ready, g + 1)
                for m in range(KC // 2):
                    b = m % 2
                    pe.wait_ge(m_taken[b], g * BANK_JOBS + m // 2 + 1)
                    for kk in range(2):
                        k = 2 * m + kk
                        for a in range(TT):
                            last = mm(psum[6 + b][:, kk * T:(kk + 1) * T], x1[:, a, k * P:(k + 1) * P],
                                      hot[:, a, :, :].rearrange("p e s -> p (e s)"), a == 0, a == TT - 1)
                    last.then_inc(m_full[b], 1)
                for le in range(GRP):
                    count = pe.value_load(counts[0:1, bass.ds(g * GRP + le, 1)], min_val=0, max_val=T)
                    expert_pe(pe, mm, g, le, count)

        def expert_act(act, g, le, count):
            ne = g * GRP + le

            def take_turned(r, j):
                out = hidT[:, r, 4 * j:4 * j + 4, :].rearrange("p (c a) s -> p a c s", c=2)
                return act.activation(out, psum[5][:, 0:2 * P].rearrange("p (a c s) -> p a c s", a=2, c=2), ACT.Copy)

            def extra(r, sec):
                xp, xa, xd = x_pe[r], x_act[r], x_dve[r]
                bp, ba, bd = ne * X_PE, ne * X_ACT, ne * X_DVE
                if sec == "A":
                    for half in range(2):
                        act.wait_ge(xp, bp + 1 + half)
                        for k in range(8):
                            kk = 8 * half + k
                            ins = act.activation(xx[r - 1][:, kk, :], psum[1 + r][:, k * CAP:(k + 1) * CAP], ACT.Identity,
                                                 scale=modcol[:, 2 * KC + kk:2 * KC + kk + 1],
                                                 bias=modcol[:, 3 * KC + kk:3 * KC + kk + 1])
                        ins.then_inc(xa, 1)
                    act.wait_ge(xp, bp + 3)
                    act.activation(back[:, r, :, :].rearrange("p a t -> p (a t)"), psum[5][:, 0:2 * P], ACT.Copy)\
                       .then_inc(xa, 1)
                    act.wait_ge(xa, ba + 3)
                elif sec in "BD":
                    n = 4 if sec == "B" else 6
                    act.wait_ge(xp, bp + n)
                    act.activation(hidx[r], psum[1 + r][:, 0:256], ACT.Silu).then_inc(xa, 1)
                    act.wait_ge(xa, ba + n)
                elif sec in "CE":
                    act.wait_ge(xp, bp + (5 if sec == "C" else 7))
                    take_turned(r, 0 if sec == "C" else 1).then_inc(xa, 1)
                    act.wait_ge(xa, ba + (5 if sec == "C" else 7))
                act.sem_inc(extra_end["act"], 1)

            def extras(sec):
                if not ACT_SEC[sec]:
                    return
                for least, rs in ((CAP, (1,)), (2 * CAP, (2, 3))):
                    with act.If(count > least):
                        for r in rs:
                            extra(r, sec)
                    with act.Else():
                        for r in rs:
                            act.sem_inc(x_act[r], ACT_SEC[sec])

            act.wait_ge(t_full, ne * 3 + 1)
            act.activation(back[:, 0, :, :].rearrange("p a t -> p (a t)"), psum[5][:, 0:2 * P], ACT.Copy)\
               .then_inc(t_taken, 1)
            extras("A")
            for j, (one, two) in enumerate((("B", "C"), ("D", "E"))):
                extras(one)
                act.wait_ge(h_full, ne * 2 + 1 + j)
                act.activation(silu_g[j], psum[j][:, 0:256], ACT.Silu).then_inc(h_silu, 1)
                extras(two)
                act.wait_ge(t_full, ne * 3 + 2 + j)
                take_turned(0, j).then_inc(t_taken, 1)
            extras("F")

        @block.scalar
        def _(act):
            def load(dst, src, s):
                act.dma_start(dst, src).then_inc(s, 16)

            load(cT[:, :], c_T_d, s_c)
            load(rel[0:BUCKETS, :], rel_bias_d, s_rel)
            load(buckets, buckets_d, s_rel)
            load(square[:, :], square_d, s_const)
            load(ada_bias[0:MOD * 4, :], ada_b_d, s_const)
            load(region_a[:, :], x_T_d, s_xT)
            act.wait_ge(s_c, 16)
            act.activation(condT[:, :], cT[:, :], ACT.Silu).then_inc(s_cond, 1)
            act.wait_ge(s_toep, 1)
            act.activation(toe_row, psum[4][0:H, 0:TOE], ACT.Copy).then_inc(s_toer, 1)
            act.wait_ge(s_toer, 1)
            load(toe_dram[:, :, :], toe_row.rearrange("h (o j) -> h o j", o=1).to_broadcast([H, P, TOE]), s_toed)
            load(sgu_wT[:, :], sgu_wT_d, s_sguw)
            load(sgu_g, sgu_g_d.to_broadcast([P, G * P]), s_sgubc)
            load(sgu_b, sgu_b_d.to_broadcast([P, G * P]), s_sgubc)
            load(sgu_bias[:, :], sgu_bias_d, s_sgubc)
            load(slots[:, :], slots_d, s_router)
            load(router_w[:, :].rearrange("p (k e) -> p k e", e=NE), router_w_d.rearrange("(k p) e -> p k e", p=P), s_router)
            load(router_b, router_b_d.to_broadcast([P, NE]), s_router)
            act.wait_ge(s_toed, 16)
            blocks = bass.AP(toe_dram[:, :, :].tensor, P - 1, [[TOE - 1, P], [P * TOE, H], [1, T]])
            load(toep, blocks, s_toe)

            def evict(i, m):
                kind, j = W_UNITS[i]
                job = JOB[i, m]
                act.wait_ge(job_full, job + 1)
                src = psum[job % 4][:, :]
                pair = src.rearrange("p (c t) -> p c t", c=2)
                chunk = 4 * j + 2 * m
                if kind == "q":
                    ins = act.activation(qT[:, chunk:chunk + 2, :], pair, ACT.Copy)
                elif kind == "k":
                    ins = act.activation(kT[:, chunk:chunk + 2, :], pair, ACT.Copy)
                elif kind == "v":
                    ins = act.activation(v[:, m, j * UW:(j + 1) * UW], src, ACT.Copy)
                elif kind == "u":
                    ins = act.activation(uT[:, chunk:chunk + 2, :], pair, ACT.Gelu_apprx_tanh)
                elif kind == "z":
                    ins = act.activation(zv[:, m, j * UW:(j + 1) * UW], src, ACT.Gelu_apprx_tanh)
                else:
                    b = int(kind == "gate1")
                    if j == 0:
                        act.wait_ge(o_full, H)
                    else:
                        act.wait_ge(dve_emptied, 4 * j)
                    ins = act.activation(gates[:, 2 * m:2 * m + 2, b, :], pair, ACT.Sigmoid)
                ins.then_inc(act_emptied, 1)

            def ada_take(a):
                m, j = ADA_UNITS[a]
                act.wait_ge(ada_sum, a + 1)
                if m == G1:
                    ins = act.activation(g1b[:, j * UW:(j + 1) * UW], psum[7][:, :], ACT.Copy)
                elif m == G2:
                    c, q = j % 2, j // 2
                    half = slice(64 * c, 64 * c + 64)
                    ins = act.activation(g2x[half, q * UW:(q + 1) * UW], psum[7][half, :], ACT.Copy)
                else:
                    col = (2 if m == SC2 else 3) * KC + 4 * j
                    ins = act.activation(modcol[:, col:col + 4], psum[7][:, 0:4], ACT.Copy)
                ins.then_inc(ada_outa, 1)

            def att(s):
                if s < H:
                    pr = prob[s % 2]
                    act.wait_ge(s_max, s + 1)
                    act.activation(pr[:, 0:P], pr[:, 0:P], ACT.Exp, bias=nmax2[s % 2][:, 0:1],
                                   accum_out=rsum2[s % 2][:, 0:1])
                    act.activation(pr[:, P:3 * P], pr[:, P:3 * P], ACT.Exp, bias=nmax2[s % 2][:, 1:2],
                                   accum_out=rsum2[s % 2][:, 1:2]).then_inc(s_exp, 1)
                if s >= 2:
                    act.wait_ge(o_full, s - 1)
                    act.activation(attT[:, s - 2, :], psum[6][:, 0:T], ACT.Copy).then_inc(o_taken, 1)

            for step in SCHEDULE:
                if step[0] == "part" and step[3] == 1 and not by_dve(JOB[step[1], step[2]]):
                    evict(step[1], step[2])
                elif step[0] == "att":
                    att(step[1])
                elif step[0] == "ada":
                    ada_take(step[1])
                elif step[0] == "norm":
                    act.wait_ge(z_var, 1)
                    act.activation(zrstd, zmv[:, :, 1], ACT.Sqrt, bias=eps[:, :]).then_inc(z_std, 1)
                if step == ("mix", 3):
                    act.wait_ge(sc_taken, H)
                    act.wait_ge(z_ready, 1)
                    load(x1, x_tok_d.rearrange("(a p) d -> p a d", p=P), s_x)
                    act.wait_ge(mix_full, 4)
                    load(ln1g, ln1_g_d.to_broadcast([P, D]), s_ln1)
            act.wait_ge(job_full, JOB[W_UNITS.index(("branch", 3)), 3] + 1)
            load(ln1b, ln1_b_d.to_broadcast([P, D]), s_ln1)

            def roots(first):
                for a in range(TT):
                    act.wait_ge(l_var, first + a + 1)
                    act.activation(lrstd[:, a:a + 1], lmv[:, a, 1:2], ACT.Sqrt, bias=eps[:, :]).then_inc(l_std, 1)

            roots(0)
            act.wait_ge(x1_ready, TT)
            act.wait_ge(s_sc2, 1)
            for m in range(KC // 2):
                act.wait_ge(xt_full, m + 1)
                for kk in range(2):
                    k = 2 * m + kk
                    ins = act.activation(hmT[:, k, :], psum[6 + m % 2][:, kk * T:(kk + 1) * T], ACT.Identity,
                                         scale=modcol[:, 2 * KC + k:2 * KC + k + 1],
                                         bias=modcol[:, 3 * KC + k:3 * KC + k + 1])
                ins.then_inc(xt_taken, 1)
            act.wait_ge(lg_full, 1)
            act.activation(lgT, psum[5][0:NE, 0:T], ACT.Copy).then_inc(lg_copied, 1)
            act.wait_ge(lg_sub, 1)
            act.activation(aff, aff, ACT.Exp).then_inc(lg_exp, 1)
            for a in range(TT):
                act.activation(acc[:, a, :], x1[:, a, :], ACT.Copy, scale=ALPHA).then_inc(acc_ready, 1)
            act.wait_ge(routed, 1)

            with act.Fori(0, NE // GRP) as g:
                for m in range(KC // 2):
                    b = m % 2
                    act.wait_ge(m_full[b], g * BANK_JOBS + m // 2 + 1)
                    for kk in range(2):
                        k = 2 * m + kk
                        ins = act.activation(xe[:, k, :], psum[6 + b][:, kk * T:(kk + 1) * T], ACT.Identity,
                                             scale=modcol[:, 2 * KC + k:2 * KC + k + 1],
                                             bias=modcol[:, 3 * KC + k:3 * KC + k + 1])
                    ins.then_inc(m_taken[b], 1)
                for le in range(GRP):
                    count = act.value_load(counts[0:1, bass.ds(g * GRP + le, 1)], min_val=0, max_val=T)
                    expert_act(act, g, le, count)
            roots(TT)

        @block.vector
        def _(dve):
            links = [0]

            def link(ins):
                links[0] += 1
                ins.then_inc(link_dve, 1)
                dve.wait_ge(link_dve, links[0])

            link(dve.memset(rel[BUCKETS:BUCKETS + 1, :], 1.0))
            dve.sem_inc(s_relone, 1)
            dve.wait_ge(s_cond, 1)
            dve.wait_ge(s_xT, 16)

            def ada_take(a):
                m, j = ADA_UNITS[a]
                dve.wait_ge(ada_sum, a + 1)
                dst = modcol[:, (0 if m == SC1 else KC) + 4 * j:(0 if m == SC1 else KC) + 4 * j + 4]
                ins = dve.tensor_scalar(dst, psum[7][:, 0:4], 1.0 if m == SC1 else 0.0, None, ALU.add)
                ins.then_inc(ada_out, 1)
                if m == SH1:
                    dve.wait_ge(ada_out, a + 1)
                    for k in range(4 * j, 4 * j + 4):
                        ins = dve.tensor_scalar(xmT[:, k, :], xmT[:, k, :], modcol[:, k:k + 1],
                                                modcol[:, KC + k:KC + k + 1], ALU.mult, ALU.add)
                    ins.then_inc(xm_ready, 1)

            def ada_part(a, ks):
                dst = ada_row[a % 2]
                if ks[0] == 0:
                    unit_loaded(dve, AT["ada", a])
                    if a >= 2:
                        dve.wait_ge(ada_sum, a - 1)
                w = slot(AT["ada", a]).rearrange("p (k n) -> p k n", n=UW)
                for k in ks:
                    if k == 0:
                        ins = dve.tensor_scalar(dst, w[:, 0, :], condT[:, 0:1], None, ALU.mult)
                    else:
                        ins = dve.scalar_tensor_tensor(out=dst, in0=w[:, k, :], scalar=condT[:, k:k + 1], in1=dst,
                                                       op0=ALU.mult, op1=ALU.add)
                    if k < KC - 1:
                        link(ins)
                    else:
                        ins.then_inc(ada_acc, 1)

            for a in range(ADA_FIRST):
                ada_part(a, range(KC))
                if a >= 1:
                    ada_take(a - 1)
            ada_take(ADA_FIRST - 1)

            def att(s):
                if s < H:
                    pr = prob[s % 2]
                    if s == 0:
                        dve.wait_ge(s_toe, 16)
                    dve.wait_ge(sc_full, s + 1)
                    if s >= 2:
                        dve.wait_ge(pt_full, s - 1)
                    dve.scalar_tensor_tensor(out=pr[:, 0:P], in0=psum[4][:, 0:P], scalar=QSCALE,
                                             in1=toep[:, s, P:T], op0=ALU.mult, op1=ALU.add)
                    ins = dve.scalar_tensor_tensor(out=pr[:, P:3 * P], in0=psum[4][:, P:3 * P], scalar=QSCALE,
                                                   in1=toep[:, s, :], op0=ALU.mult, op1=ALU.add)
                    ins.then_inc(sc_taken, 1)
                    dve.wait_ge(sc_taken, s + 1)
                    dve.tensor_reduce(nmax2[s % 2][:, 0:1], pr[:, 0:P], AX_X, ALU.max, negate=True)
                    dve.tensor_reduce(nmax2[s % 2][:, 1:2], pr[:, P:3 * P], AX_X, ALU.max, negate=True)\
                       .then_inc(s_max, 1)
                if 1 <= s <= H:
                    dve.wait_ge(pt_full, s)
                    if s >= 3:
                        dve.wait_ge(o_full, s - 2)
                    dve.tensor_copy(pTs[(s - 1) % 2], psum[5][:, 0:3 * P]).then_inc(pt_taken, 1)
                if s < H:
                    dve.wait_ge(s_exp, s + 1)
                    link(dve.reciprocal(rinv, rsum2[s % 2]))
                    dve.tensor_scalar(pr[:, 0:P], pr[:, 0:P], rinv[:, 0:1], None, ALU.mult)
                    ins = dve.tensor_scalar(pr[:, P:3 * P], pr[:, P:3 * P], rinv[:, 1:2], None, ALU.mult)
                    ins.then_inc(p_norm, 1)

            def gating_norm():
                dve.wait_ge(act_emptied, 20)
                dve.wait_ge(s_sgubc, 48)
                for a in range(TT):
                    for q in range(G):
                        ins = dve.bn_stats(zstat[:, a * G + q, :], zv[:, a, q * P:(q + 1) * P])
                link(ins)
                for n in range(TT * G):
                    ins = dve.bn_aggr(zmv[:, n, :], zstat[:, n, :])
                ins.then_inc(z_var, 1)
                dve.wait_ge(z_std, 1)
                link(dve.reciprocal(zrstd, zrstd))
                for a in range(TT):
                    for q in range(G):
                        n = a * G + q
                        z = zv[:, a, q * P:(q + 1) * P]
                        ins = dve.tensor_scalar(z, z, zmv[:, n, 0:1], zrstd[:, n:n + 1], ALU.subtract, ALU.mult)
                link(ins)
                for a in range(TT):
                    ins = dve.tensor_tensor(zv[:, a, :], zv[:, a, :], sgu_g, ALU.mult)
                link(ins)
                for a in range(TT):
                    ins = dve.tensor_tensor(zv[:, a, :], zv[:, a, :], sgu_b, ALU.add)
                ins.then_inc(z_ready, 1)

            def gated(m):
                a, half = m // 2, m % 2
                dve.wait_ge(mix_full, m + 1)
                u = uT[:, 4 * half:4 * half + 4, a * P:(a + 1) * P]
                dve.tensor_tensor(u, u, psum[4 + m % 3][:, :].rearrange("p (q t) -> p q t", q=4), ALU.mult)\
                   .then_inc(mix_taken, 1)

            def evict(i, m):
                kind, j = W_UNITS[i]
                job = JOB[i, m]
                dve.wait_ge(job_full, job + 1)
                bank = psum[job % 4][:, :]
                t = tmp[job % 2]
                if kind == "branch":
                    dve.wait_ge(act_emptied, evictions(JOB[i - 1, m // 2]))
                    ins = dve.tensor_tensor(t, bank, gates[:, m, :, :].rearrange("p b t -> p (b t)"), ALU.mult)
                    ins.then_inc(dve_emptied, 1)
                    dve.wait_ge(dve_emptied, evictions(job))
                    dve.tensor_tensor(mixT[:, 4 * j + m, :], t[:, 0:T], t[:, T:2 * T], ALU.add).then_inc(mix_ready, 1)
                else:
                    cols = slice(j * UW, (j + 1) * UW)
                    if j == 0 and m == 0:
                        dve.wait_ge(s_x, 16)
                    dve.tensor_tensor(t, bank, g1b[:, cols], ALU.mult).then_inc(dve_emptied, 1)
                    dve.wait_ge(dve_emptied, evictions(job))
                    link(dve.scalar_tensor_tensor(out=x1[:, m, cols], in0=x1[:, m, cols], scalar=ALPHA, in1=t,
                                                  op0=ALU.mult, op1=ALU.add))

            for step in SCHEDULE:
                if step[0] == "part" and step[3] == 1 and by_dve(JOB[step[1], step[2]]):
                    evict(step[1], step[2])
                elif step[0] == "att":
                    att(step[1])
                elif step[0] == "adapart":
                    ada_part(*step[1:])
                elif step[0] == "norm":
                    gating_norm()
                elif step[0] == "mix":
                    gated(step[1])

            def norm(x, gamma, beta, first, done):
                for a in range(TT):
                    for q in range(4):
                        ins = dve.bn_stats(lstat[:, a, q, :], x[:, a, q * 512:(q + 1) * 512])
                    link(ins)
                    dve.bn_aggr(lmv[:, a, :], lstat[:, a, :, :].rearrange("p n s -> p (n s)")).then_inc(l_var, 1)
                for a in range(TT):
                    dve.wait_ge(l_std, first + a + 1)
                    link(dve.reciprocal(lrstd[:, a:a + 1], lrstd[:, a:a + 1]))
                    link(dve.tensor_scalar(x[:, a, :], x[:, a, :], lmv[:, a, 0:1], lrstd[:, a:a + 1],
                                           ALU.subtract, ALU.mult))
                    link(dve.tensor_tensor(x[:, a, :], x[:, a, :], gamma, ALU.mult))
                    dve.tensor_tensor(x[:, a, :], x[:, a, :], beta, ALU.add).then_inc(done, 1)

            dve.wait_ge(ada_outa, len(ADA_UNITS) - ADA_FIRST)
            dve.tensor_scalar(modcol[:, 2 * KC:3 * KC], modcol[:, 2 * KC:3 * KC], 1.0, None, ALU.add).then_inc(s_sc2, 1)
            dve.wait_ge(s_ln1, 32)
            norm(x1, ln1g, ln1b, 0, x1_ready)

            def tiles(t, n):
                return t.rearrange("p (a e) -> p a e", e=n)

            dve.wait_ge(s_router, 48)
            dve.wait_ge(lg_turned, 1)
            lg = psum[4][:, 0:2 * NE]
            link(dve.tensor_tensor(tiles(aff, NE), tiles(lg, NE),
                                   router_b.rearrange("p (a e) -> p a e", a=1).to_broadcast([P, TT, NE]), ALU.add))
            link(dve.tensor_reduce(gsc[:, 0:TT], tiles(aff, NE), AX_X, ALU.max))
            for a in range(TT):
                ins = dve.tensor_scalar(aff[:, a * NE:(a + 1) * NE], aff[:, a * NE:(a + 1) * NE], gsc[:, a:a + 1],
                                        None, ALU.subtract)
            ins.then_inc(lg_sub, 1)
            dve.wait_ge(lg_exp, 1)
            link(dve.tensor_reduce(gsc[:, 0:TT], tiles(aff, NE), AX_X, ALU.add))
            link(dve.reciprocal(gsc[:, 2:2 + TT], gsc[:, 0:TT]))
            for a in range(TT):
                ins = dve.tensor_scalar(aff[:, a * NE:(a + 1) * NE], aff[:, a * NE:(a + 1) * NE],
                                        gsc[:, 2 + a:3 + a], None, ALU.mult)
            link(ins)

            def ranks(out, val, buf, n):
                val = val.rearrange("p (n j) -> p n j", j=4)
                c = buf.rearrange("p (n i j) -> p n i j", i=4, j=4)
                link(dve.memset(buf, 0.0))
                for i in range(4):
                    if i > 0:
                        ins = dve.tensor_tensor(c[:, :, i, 0:i], val[:, :, i:i + 1].to_broadcast([P, n, i]),
                                                val[:, :, 0:i], ALU.is_gt)
                    if i < 3:
                        ins = dve.tensor_tensor(c[:, :, i, i + 1:4], val[:, :, i:i + 1].to_broadcast([P, n, 3 - i]),
                                                val[:, :, i + 1:4], ALU.is_ge)
                link(ins)
                link(dve.tensor_reduce(out.rearrange("p (n j) -> p n j", j=4), c.rearrange("p n i j -> p n j i"),
                                       AX_X, ALU.add))

            ranks(rank, aff, cmp_, TT * NG)
            link(dve.tensor_scalar(sel, rank, 1.5, None, ALU.is_lt))
            link(dve.tensor_tensor(best, sel, aff, ALU.mult))
            link(dve.tensor_reduce(gsc, best.rearrange("p (n j) -> p n j", j=4), AX_X, ALU.add))
            ranks(grank, gsc, gcmp, TT)
            link(dve.tensor_scalar(grank, grank, 0.5, None, ALU.is_lt))
            in_best = grank.rearrange("p (n o) -> p n o", o=1).to_broadcast([P, TT * NG, 4])
            dve.tensor_tensor(mask.rearrange("p (n j) -> p n j", j=4), sel.rearrange("p (n j) -> p n j", j=4),
                              in_best, ALU.mult).then_inc(mask_ready, 1)
            link(dve.tensor_tensor(best.rearrange("p (n j) -> p n j", j=4), best.rearrange("p (n j) -> p n j", j=4),
                                   in_best, ALU.mult))
            link(dve.tensor_reduce(gsc[:, 0:TT], tiles(best, NE), AX_X, ALU.add))
            link(dve.reciprocal(gsc[:, 2:2 + TT], gsc[:, 0:TT]))
            for a in range(TT):
                ins = dve.tensor_scalar(wts[:, a * NE:(a + 1) * NE], best[:, a * NE:(a + 1) * NE],
                                        gsc[:, 2 + a:3 + a], None, ALU.mult)
            link(ins)
            dve.wait_ge(place_full, 1)
            link(dve.scalar_tensor_tensor(out=place, in0=psum[5][:, 0:2 * NE], scalar=-FAR, in1=mask,
                                          op0=ALU.add, op1=ALU.mult))
            link(dve.tensor_scalar(place, place, FAR, None, ALU.add))
            dve.tensor_copy(counts[:, :], psum[5][:, 2 * NE:3 * NE]).then_inc(routed, 1)
            dve.wait_ge(routed, 1)
            dve.wait_ge(acc_ready, TT)
            dve.sem_inc(y_ready, 2)
            dve.sem_inc(m_taken[0], 1)
            dve.sem_inc(m_taken[1], 1)
            dve.sem_inc(t_taken, 1)

            slot_no = slots[:, :].rearrange("p (r c s) -> p r c s", r=XT, c=2)
            with dve.Fori(0, NE // GRP) as g:
                def chosen(e, a):
                    return place.rearrange("p (a e) -> p a e", a=TT)[:, a, bass.ds(e, 1)]

                def weight(e, a):
                    return wts.rearrange("p (a e) -> p a e", a=TT)[:, a, bass.ds(e, 1)]

                for le in range(GRP):
                    for a in range(TT):
                        ins = dve.tensor_scalar(hot[:, a, le, :], slot_no[:, 0, 0, :], chosen(g * GRP + le, a), None,
                                                ALU.is_equal)
                ins.then_inc(hot_ready, 1)
                for le in range(GRP):
                    count = dve.value_load(counts[0:1, bass.ds(g * GRP + le, 1)], min_val=0, max_val=T)
                    ne = g * GRP + le
                    for a in range(TT):
                        ins = dve.tensor_scalar(hotw[:, a, :, :], slot_no[:, 0, :, :], chosen(ne, a), weight(ne, a),
                                                ALU.is_equal, ALU.mult)
                    ins.then_inc(hotw_ready, 1)

                    def extra(r, sec):
                        xp, xa, xd = x_pe[r], x_act[r], x_dve[r]
                        bp, ba, bd = ne * X_PE, ne * X_ACT, ne * X_DVE
                        if sec == "A":
                            for a in range(TT):
                                dve.tensor_scalar(hotx[:, r, a, :], slot_no[:, r, 0, :], chosen(ne, a), None,
                                                  ALU.is_equal)
                                ins = dve.tensor_scalar(hotwx[:, a, :, :], slot_no[:, r, :, :], chosen(ne, a),
                                                        weight(ne, a), ALU.is_equal, ALU.mult)
                            ins.then_inc(xd, 1)
                            dve.wait_ge(xp, bp + 3)
                            dve.wait_ge(xd, bd + 1)
                        elif sec in "BD":
                            dve.wait_ge(xa, ba + (4 if sec == "B" else 6))
                            dve.tensor_tensor(hidx[r], hidx[r], psum[1 + r][:, 256:512], ALU.mult).then_inc(xd, 1)
                            dve.wait_ge(xd, bd + (2 if sec == "B" else 3))
                        elif sec == "F":
                            for q in range(2):
                                dve.wait_ge(xp, bp + 8 + 5 * q)
                                dve.tensor_tensor(ysbx, psum[1 + r][:, :], g2x[:, q * UW:(q + 1) * UW], ALU.mult)\
                                   .then_inc(xd, 1)
                                for a in range(TT):
                                    for c in range(2):
                                        n = 2 * a + c
                                        dve.wait_ge(xp, bp + 9 + 5 * q + n)
                                        add(psum[6 + c], q, a, c).then_inc(xd, 1)
                                        dve.wait_ge(xd, bd + 5 + 5 * q + n)
                        dve.sem_inc(extra_end["dve"], 1)

                    def extras(sec):
                        if not DVE_SEC[sec]:
                            return
                        for least, rs in ((CAP, (1,)), (2 * CAP, (2, 3))):
                            with dve.If(count > least):
                                for r in rs:
                                    extra(r, sec)
                            with dve.Else():
                                for r in rs:
                                    dve.sem_inc(x_dve[r], DVE_SEC[sec])

                    def add(bank, q, a, c):
                        dst = acc[:, a, q * 1024 + c * 512:q * 1024 + (c + 1) * 512]
                        return dve.tensor_tensor(dst, bank[:, :], dst, ALU.add)

                    def scale(q):
                        dve.wait_ge(y_full, ne * 2 + 1 + q)
                        dve.tensor_tensor(ysb[q], psum[q][:, :], g2x[:, q * UW:(q + 1) * UW], ALU.mult)\
                           .then_inc(y_ready, 1)

                    extras("A")
                    for j, (one, two) in enumerate((("B", "C"), ("D", "E"))):
                        extras(one)
                        dve.wait_ge(h_silu, ne * 2 + 1 + j)
                        dve.tensor_tensor(hid[j], silu_g[j], psum[j][:, 256:512], ALU.mult).then_inc(hid_ready, 1)
                        extras(two)
                    scale(0)
                    extras("F")
                    scale(1)
                    for q in range(2):
                        for a in range(TT):
                            for c in range(2):
                                dve.wait_ge(m_full[c], g * BANK_JOBS + 4 * (le + 1) + 2 * q + a + 1)
                                add(psum[6 + c], q, a, c).then_inc(m_taken[c], 1)
                    for c in range(2):
                        dve.wait_ge(m_taken[c], g * BANK_JOBS + 4 * (le + 2) + 1)

            dve.wait_ge(s_ln2, 32)
            norm(acc, ln2g, ln2b, TT, out_ready)


_OUT = (1, T, D)


def kernel(**inputs):
    import numpy as np
    import concourse.bacc as bacc
    from concourse.bass_utils import run_bass_kernel_spmd

    a = {k: np.asarray(v) for k, v in inputs.items()}

    square = np.zeros((P, 2 * P), np.float32)
    square[:, :P] = np.eye(P)
    square[:, P:] = np.triu(np.ones((P, P)), 1)
    slots = np.broadcast_to(np.arange(T, dtype=np.float32).reshape(1, XT, 1, CAP), (P, XT, 2, CAP)).reshape(P, -1)
    buckets = np.zeros((BUCKETS + 1, TOE), np.float32)
    for j in range(TOE):
        dist = T - 1 - j
        times = sum(dist >= 0 and dist % d == 0 and dist <= w for w, d in PATTERNS)
        buckets[BUCKETS, j] = np.log(times) if times else -1e30
        if times:
            half = BUCKETS // 2
            far = half + int(np.log(np.float32(max(dist, 1)) / np.float32(half))
                             / np.float32(np.log(2048 / half)) * np.float32(BUCKETS - half))
            buckets[dist if dist < half else min(far, BUCKETS - 1), j] = 1.0

    row = lambda t: t.reshape(1, -1)
    arrays = {
        "x_tok": a["x"][0],
        "x_T": a["x"][0].T.reshape(KC, P, T).transpose(1, 0, 2).reshape(P, KC * T),
        "c_T": a["c"].reshape(KC, P).T,
        "rel_bias": a["rel_bias"],
        "router_w": a["router_w"],
        "router_b": row(a["router_b"]),
        "ada_w": a["ada_w"][0],
        "ada_b": a["ada_b"].reshape(MOD * 4, UW),
        "w_in": a["w_in"][0],
        "sgu_g": row(a["sgu_ln_g"]),
        "sgu_b": row(a["sgu_ln_b"]),
        "sgu_wT": a["sgu_w"][0].transpose(2, 0, 1).reshape(P, G * P),
        "sgu_bias": a["sgu_b"][0],
        "w_branch": a["w_branch"].reshape(D, D),
        "w_out": a["w_out"][0],
        "ln1_g": row(a["ln1_g"]), "ln1_b": row(a["ln1_b"]),
        "ln2_g": row(a["ln2_g"]), "ln2_b": row(a["ln2_b"]),
        "w_gate": a["exp_w_gate"][0], "w_up": a["exp_w_up"][0], "w_down": a["exp_w_down"][0],
        "square": square, "slots": slots, "buckets": buckets,
    }
    arrays = {k: np.ascontiguousarray(t) for k, t in arrays.items()}
    nc = bacc.Bacc("TRN2", target_bir_lowering=False, num_devices=1, dynamic_dma_scratch_size=1024)
    args = {k + "_d": nc.dram_tensor("in_" + k, t.shape, F32, kind="ExternalInput").ap() for k, t in arrays.items()}
    out = nc.dram_tensor("out", (T, D), F32, kind="ExternalOutput").ap()
    program(nc, out_d=out, **args)
    r = run_bass_kernel_spmd(nc, [{"in_" + k: t for k, t in arrays.items()}], core_ids=[0])
    return r.results[0]["out"].reshape(_OUT)
```

```python
from contextlib import ExitStack

import concourse.bass as bass
from concourse import mybir

F32 = mybir.dt.float32
I32 = mybir.dt.int32
ALU = mybir.AluOpType
ACT = mybir.ActivationFunctionType
AX_X = mybir.AxisListType.X

P = 128
D = 2048
T = 256
TT = T // P
KC = D // P
H = 8
G = 8
MOD = 6
NE = 16
NG = 4
F = 1024
PATTERNS = ((128, 1), (512, 4), (2048, 16))
BUCKETS = 32
ALPHA = 2.0 ** 0.25
EPS = 1e-5
QSCALE = float(P) ** -0.5
UW = 512
RING = 3
SLOT = KC * UW
CAP = 64
EXTRA = {1: (64, 32, 2), 2: (96, 32, 3), 3: (128, 64, 4), 4: (192, 64, 7)}
LEVELS = ((1,), (2,), (3, 4))
GRP = 4
TOE = 384
FAR = 1024.0

W_UNITS = ([("v", 0), ("v", 1), ("z", 0), ("q", 0), ("q", 1), ("k", 0), ("k", 1), ("u", 0), ("u", 1), ("z", 1)]
           + [(kind, j) for j in range(4) for kind in ("gate0", "gate1", "branch")]
           + [("out", j) for j in range(4)])
IN_COL = {"q": 0, "k": 1024, "v": 2048, "u": 3072, "z": 4096, "gate0": 5120, "gate1": 7168}
SH1, SC1, G1, SH2, SC2, G2 = range(MOD)
ADA_UNITS = [(m, j) for j in range(4) for m in (SC1, SH1)] + [(m, j) for m in (G1, SC2, SH2, G2) for j in range(4)]
ADA_FIRST = 8
BY_ROWS = 3
STREAM = []
for _r in range(4):
    STREAM += [("ada", 2 * _r), ("ada", 2 * _r + 1), ("rows", _r)]
for _i in range(BY_ROWS, len(W_UNITS)):
    STREAM.append(("w", _i))
    if ADA_FIRST + _i - BY_ROWS < len(ADA_UNITS):
        STREAM.append(("ada", ADA_FIRST + _i - BY_ROWS))
AT = {u: n for n, u in enumerate(STREAM)}
NFRONT = len(STREAM)
NW = len(W_UNITS)
E_UNITS = 6
JOBS = [(i, m) for i, (kind, _) in enumerate(W_UNITS) for m in range(4 if kind == "branch" else 2)]
JOB = {im: n for n, im in enumerate(JOBS)}


def by_dve(n):
    return W_UNITS[JOBS[n][0]][0] in ("branch", "out")


def job_bank(n):
    return n if n < 2 * BY_ROWS else n % 4


def evictions(n):
    return sum(by_dve(k) == by_dve(n) for k in range(n + 1))


SCHEDULE = []
ADA_ROWS = {(1, 0): range(0, 6), (1, 1): range(6, 12), (0, 0): range(12, KC)}
_att = 0
for _i, (_kind, _j) in list(enumerate(W_UNITS))[BY_ROWS:]:
    for _m in range(4 if _kind == "branch" else 2):
        for _h in range(2):
            SCHEDULE.append(("part", _i, _m, _h))
            _a = ADA_FIRST + _i - BY_ROWS - (_m == 0)
            if (_m, _h) in ADA_ROWS and ADA_FIRST <= _a < len(ADA_UNITS):
                SCHEDULE.append(("adapart", _a, ADA_ROWS[_m, _h]))
            if _i >= 7 and _att < H + 2:
                SCHEDULE.append(("att", _att))
                _att += 1
    if 1 <= _i - BY_ROWS <= len(ADA_UNITS) - ADA_FIRST:
        SCHEDULE.append(("ada", ADA_FIRST + _i - BY_ROWS - 1))
    if _i == 9:
        SCHEDULE.append(("norm",))
    if _i == 11:
        SCHEDULE += [("mix", m) for m in range(4)]

def strips(x):
    return P // (CAP if x == 0 else EXTRA[x][1])


def rounds(x):
    return 4 // strips(x)


def pe_count(x, event):
    a = 2 * rounds(x) + 1
    return {"oneT": a, "h0": a + 1, "t0": a + 2, "h1": a + 3, "t1": a + 4, "y0": a + 5, "s0": a + 6, "y1": a + 7,
            "all": a + 8}[event]


def act_count(x, event):
    a = rounds(x) + 1
    return {"oneT": a, "h0": a + 1, "t0": a + 2, "h1": a + 3, "all": a + 4}[event]


def dve_count(x, event):
    a = 2 * rounds(x) + 1
    return {"tokens": a, "h0": a + 1, "h1": a + 2, "y0": a + 3, "s0": a + 4, "y1": a + 5, "all": a + 6}[event]


BANK_JOBS = 4 + 4 * GRP


def program(nc, x_tok_d, x_T_d, c_T_d, rel_bias_d, router_w_d, router_b_d, ada_w_d, ada_b_d, w_in_d,
            sgu_g_d, sgu_b_d, sgu_wT_d, sgu_bias_d, w_branch_d, w_out_d, ln1_g_d, ln1_b_d, ln2_g_d, ln2_b_d,
            w_gate_d, w_up_d, w_down_d, square_d, slots_d, buckets_d, out_d):
    with ExitStack() as ctx:
        def sb(name, cols, dt=F32, parts=P):
            return ctx.enter_context(nc.sbuf_tensor(name, [parts, cols], dt))

        def sem(name):
            return ctx.enter_context(nc.semaphore(name))

        ring = sb("ring", RING * SLOT)
        region_a = sb("region_a", KC * T)
        region_b = sb("region_b", KC * T)
        region_c = sb("region_c", 2048)
        region_d = sb("region_d", 2048)
        region_e = sb("region_e", 2048)
        region_f = sb("region_f", 2048)
        region_x = sb("region_x", TT * D)
        g1b = sb("g1b", D)
        g2n = sb("g2n", UW)
        g2x = sb("g2x", 2 * UW)
        sgu_wT = sb("sgu_wT", G * P)
        work = sb("work", 1024)
        work2 = sb("work2", 1024)
        square = sb("square", 2 * P)
        slots = sb("slots", T)
        ones = sb("ones", P)
        eps = sb("eps", 1)
        condT = sb("condT", KC)
        cond_pad = sb("cond_pad", KC * 32)
        cT = sb("cT", KC)
        ada_bias = sb("ada_bias", UW)
        sgu_bias = sb("sgu_bias", P, parts=G)
        small = sb("small", 640)
        modcol = sb("modcol", 4 * KC)
        router_w = sb("router_w", KC * NE)
        counts = sb("counts", NE, I32)

        psum = [ctx.enter_context(nc.psum_tensor(f"bank{i}", [P, 512], F32)) for i in range(8)]

        def slot(n):
            return ring[:, (n % RING) * SLOT:(n % RING + 1) * SLOT]

        ident = square[:, 0:P]
        upper = square[:, P:2 * P]
        xmT = region_a[:, :].rearrange("p (k t) -> p k t", t=T)
        acc = region_a[:, :].rearrange("p (a d) -> p a d", a=TT)
        qT = region_b[:, 0:H * T].rearrange("p (h t) -> p h t", t=T)
        kT = region_b[:, H * T:2 * H * T].rearrange("p (h t) -> p h t", t=T)
        mixT = region_b[:, :].rearrange("p (k t) -> p k t", t=T)
        hmT = mixT
        xe = mixT
        v = region_c[:, :].rearrange("p (a n) -> p a n", a=TT)
        gates = region_c[:, :].rearrange("p (c b t) -> p c b t", c=4, b=2)
        uT = region_d[:, :].rearrange("p (g t) -> p g t", t=T)
        zv = region_e[:, :].rearrange("p (a n) -> p a n", a=TT)
        attT = region_f[:, :].rearrange("p (h t) -> p h t", t=T)
        toep = region_x[:, 0:H * T].rearrange("p (h s) -> p h s", s=T)
        sgu_g = region_x[:, 2048:3072]
        sgu_b = region_x[:, 3072:4096]
        x1 = region_x[:, :].rearrange("p (a d) -> p a d", a=TT)
        ln1g, ln1b = region_e[:, :], region_d[:, :]
        ln2g = slot(NFRONT + NE * E_UNITS - 3)[:, 0:D]
        ln2b = slot(NFRONT + NE * E_UNITS - 3)[:, D:2 * D]
        xx = [None] + [t[:, a:a + KC * n].rearrange("p (k s) -> p k s", s=n)
                       for t, a, n in ((region_c, 0, 32), (region_c, 512, 32), (region_c, 1024, 64), (region_d, 0, 64))]
        hot = region_e[:, 0:TT * GRP * CAP].rearrange("p (a e s) -> p a e s", a=TT, e=GRP)
        hotw = region_e[:, 512:768].rearrange("p (a n) -> p a n", a=TT)
        hotx = region_e[:, 768:896].rearrange("p (a s) -> p a s", a=TT)
        hotwx = region_e[:, 896:1152].rearrange("p (a n) -> p a n", a=TT)
        passing = region_e[:, 1152:1664]
        back = [t[:, a:a + T].rearrange("p (a t) -> p a t", a=TT)
                for t, a in [(region_d, 1024 + T * r) for r in range(4)] + [(region_e, 1664)]]
        hidT = [region_f[:, a:a + 8 * n].rearrange("p (k s) -> p k s", s=n)
                for a, n in ((0, 64), (512, 32), (768, 32), (1024, 64), (1536, 64))]
        ysb = [sgu_wT[:, 0:512], sgu_wT[:, 512:1024]]
        silu_g = [work[:, 0:256], work[:, 256:512]]
        hid = [work2[:, 0:256], work2[:, 256:512]]
        hidx = [None, work[:, 512:640], work[:, 640:768], work[:, 768:1024], work2[:, 512:768]]
        tmp = [work[:, 0:512], work[:, 512:1024]]
        prob = [work2[:, 0:384], work2[:, 384:768]]
        pT = sb("pT", 2 * 3 * P)
        pTs = [pT[:, 0:3 * P], pT[:, 3 * P:]]
        ada_rows = sb("ada_rows", 2 * UW)
        ada_row = [ada_rows[:, 0:UW], ada_rows[:, UW:]]
        att_o = small[:, 0:16]
        nmax2 = [att_o[:, 0:2], att_o[:, 2:4]]
        rsum2 = [att_o[:, 4:6], att_o[:, 6:8]]
        rinv = att_o[:, 8:10]
        zstat = small[:, 16:16 + 2 * G * 6].rearrange("p (n s) -> p n s", s=6)
        zmv = small[:, 112:112 + 2 * G * 2].rearrange("p (n s) -> p n s", s=2)
        zrstd = small[:, 144:160]
        lstat = small[:, 160:160 + TT * 24].rearrange("p (a n s) -> p a n s", a=TT, s=6)
        lmv = small[:, 208:212].rearrange("p (a s) -> p a s", s=2)
        lrstd = small[:, 212:214]
        router_b = small[:, 216:232]
        lgT = work[0:NE, 0:T]
        aff = small[:, 232:264]
        wts = small[:, 264:296]
        place = small[:, 296:328]
        mask = small[:, 328:360]
        rank = small[:, 360:392]
        sel = small[:, 392:424]
        best = small[:, 424:456]
        gsc = small[:, 456:464]
        grank = small[:, 464:472]
        cmp_ = small[:, 480:608]
        gcmp = small[:, 608:640]
        toe_row = region_f[0:H, 0:TOE]
        buckets = region_f[0:BUCKETS + 1, TOE:2 * TOE]
        rel = sb("rel", H, parts=BUCKETS + 1)
        toe_dram = nc.dram_tensor("toe_dram", (H, P, TOE), F32, kind="Internal")

        loaded = [sem(f"ring_loaded{i}") for i in range(RING)]
        slot_freed = sem("slot_seen_free_by_sp")
        extra_end = {e: sem(f"extra_section_end_{e}") for e in ("pe", "act", "dve")}
        extras_added = sem("extra_tiles_added")
        used_ac = sem("first_unit_of_pair_used")
        s_c = sem("c_loaded")
        s_xT = sem("xT_loaded")
        s_const = sem("const_loaded")
        s_rel = sem("rel_loaded")
        s_sguw = sem("sguw_loaded")
        s_sgubc = sem("sgu_norm_loaded")
        s_router = sem("router_loaded")
        s_x = sem("x_loaded")
        s_ln1 = sem("ln1_loaded")
        s_ln2 = sem("ln2_loaded")
        s_toed = sem("toeplitz_stored")
        s_toe = sem("toeplitz_loaded")
        s_out = sem("out_stored")
        s_ones = sem("ones_set")
        s_relone = sem("rel_one_set")
        s_toep = sem("toeplitz_row_summed")
        s_toer = sem("toeplitz_row_ready")
        s_cond = sem("cond_ready")
        ada_mm = sem("ada_multiplied_by_pe")
        ada_acc = sem("ada_acc_ready")
        s_pad = sem("cond_pad_zeroed")
        ada_sum = sem("ada_summed")
        ada_out = sem("ada_taken_dve")
        ada_outa = sem("ada_taken_act")
        s_sc2 = sem("scale2_ready")
        xm_ready = sem("xm_ready")
        causal = sem("gating_causal")
        link_dve = sem("dve_link")
        rows_used = sem("row_block_parts_multiplied")
        job_full = sem("job_full")
        act_emptied = sem("job_emptied_act")
        dve_emptied = sem("job_emptied_dve")
        sc_full = sem("scores_full")
        sc_taken = sem("scores_taken")
        s_max = sem("row_max_ready")
        s_exp = sem("exp_ready")
        p_norm = sem("probs_ready")
        pt_full = sem("probsT_full")
        pt_taken = sem("probsT_taken")
        o_full = sem("att_full")
        o_taken = sem("att_taken")
        z_var = sem("gating_var_ready")
        z_std = sem("gating_std_ready")
        z_ready = sem("gating_v_ready")
        mix_full = sem("mixed_full")
        mix_taken = sem("mixed_taken")
        mix_ready = sem("mixT_ready")
        l_var = sem("ln_var_ready")
        l_std = sem("ln_std_ready")
        x1_ready = sem("x1_ready")
        acc_ready = sem("acc_ready")
        xt_full = sem("x1T_full")
        xt_taken = [sem("x1T_taken_act"), sem("x1T_taken_dve")]
        lg_full = sem("logitsT_full")
        lg_copied = sem("logitsT_copied")
        lg_turned = sem("logits_turned")
        lg_sub = sem("logits_shifted")
        lg_exp = sem("logits_exp")
        mask_ready = sem("mask_ready")
        place_full = sem("place_full")
        routed = sem("routed")
        hot_ready = sem("hot_ready")
        hotw_ready = sem("hotw_ready")
        t_full = sem("turned_full")
        t_taken = sem("turned_taken")
        m_full = [sem("bank6_full"), sem("bank7_full")]
        m_taken = [sem("bank6_taken"), sem("bank7_taken")]
        h_full = sem("h_full")
        h_silu = sem("h_silu")
        hid_ready = sem("hid_ready")
        y_full = sem("y_full")
        y_ready = sem("y_ready")
        x_pe = [None] + [sem(f"extra{x}_pe") for x in EXTRA]
        x_act = [None] + [sem(f"extra{x}_act") for x in EXTRA]
        x_dve = [None] + [sem(f"extra{x}_dve") for x in EXTRA]
        out_ready = sem("out_ready")

        block = ctx.enter_context(nc.Block())

        def row_parts(n):
            return (slot(n)[:, 0:8 * UW].rearrange("p (k n) -> p k n", k=4),
                    slot(n)[:, 8 * UW:12 * UW].rearrange("p (k n) -> p k n", k=4))

        def unit_loaded(eng, n):
            eng.wait_ge(loaded[n % RING], 32 * (n // RING + 1))

        def e_unit_loaded(eng, g, t):
            n = NFRONT + t
            eng.wait_ge(loaded[n % RING], g * (32 * GRP * E_UNITS // RING) + 32 * (n // RING + 1))

        def unit_used(eng, n):
            kind, i = STREAM[n]
            if kind == "w":
                eng.wait_ge(job_full, JOB[i, 3 if W_UNITS[i][0] == "branch" else 1] + 1)
            elif kind == "rows":
                eng.wait_ge(job_full, 2 * BY_ROWS)
            elif i < ADA_FIRST:
                eng.wait_ge(ada_mm, i + 1)
            else:
                eng.wait_ge(ada_acc, i + 1)

        @block.sync
        def _(sp):
            sp.dma_start(cT[:, :], c_T_d).then_inc(s_c, 16)
            for n, (kind, i) in enumerate(STREAM):
                if n >= RING and kind != "rows":
                    unit_used(sp, n - RING)
                if kind == "rows":
                    for part, (dst, kind, width) in enumerate(zip(row_parts(n), ("v", "z"), (2 * UW, UW))):
                        if i > 0:
                            sp.wait_ge(rows_used, 2 * (i - 1) + part + 1)
                        rows = w_in_d[i * UW:(i + 1) * UW, IN_COL[kind]:IN_COL[kind] + width]
                        sp.dma_start(dst, rows.rearrange("(k p) n -> p k n", p=P)).then_inc(loaded[n % RING], 16)
                    continue
                if kind == "ada":
                    m, j = ADA_UNITS[i]
                    src, col = ada_w_d, m * D + j * UW
                elif W_UNITS[i][0] == "branch":
                    src, col = w_branch_d, W_UNITS[i][1] * UW
                elif W_UNITS[i][0] == "out":
                    src, col = w_out_d, W_UNITS[i][1] * UW
                else:
                    src, col = w_in_d, IN_COL[W_UNITS[i][0]] + W_UNITS[i][1] * UW
                dst = slot(n).rearrange("p (k n) -> p k n", n=UW)
                for h in range(2):
                    rows = src[h * 1024:(h + 1) * 1024, col:col + UW].rearrange("(k p) n -> p k n", p=P)
                    sp.dma_start(dst[:, 8 * h:8 * h + 8, :], rows).then_inc(loaded[n % RING], 16)

            def load_unit(g, t):
                e, s = g * GRP + t // E_UNITS, t % E_UNITS
                n = NFRONT + t
                for h in range(2):
                    if s < 4:
                        j, half = s // 2, s % 2
                        dst = slot(n).rearrange("p (k u n) -> p k u n", k=8, u=2)[:, :, h, :]
                        src = (w_gate_d, w_up_d)[h][bass.ds(e, 1), half * 1024:(half + 1) * 1024, j * 512:(j + 1) * 512]
                    else:
                        q = s - 4
                        dst = slot(n).rearrange("p (k n) -> p k n", k=8)[:, 4 * h:4 * h + 4, :]
                        src = w_down_d[bass.ds(e, 1), h * 512:(h + 1) * 512, q * 1024:(q + 1) * 1024]
                    sp.dma_start(dst, src.rearrange("o (k p) n -> p (o k) n", p=P)).then_inc(loaded[n % RING], 16)

            def unit_multiplied(g, t):
                ne, s = g * GRP + t // E_UNITS, t % E_UNITS
                done = (used_ac, h_full, used_ac, h_full, y_full, y_full)[s]
                sp.wait_ge(done, ne * 2 + (1, 1, 2, 2, 1, 2)[s])
                sp.sem_inc(slot_freed, 1)

            for t in range(RING):
                unit_used(sp, NFRONT + t - RING)
                load_unit(0, t)
            units = GRP * E_UNITS
            with sp.Fori(0, NE // GRP - 1) as g:
                for t in range(units):
                    unit_multiplied(g, t)
                    load_unit(g, t + RING)
            for t in range(units - RING):
                unit_multiplied(NE // GRP - 1, t)
                load_unit(NE // GRP - 1, t + RING)
            unit_multiplied(NE // GRP - 1, units - RING)
            sp.dma_start(ln2g, ln2_g_d.to_broadcast([P, D])).then_inc(s_ln2, 16)
            sp.dma_start(ln2b, ln2_b_d.to_broadcast([P, D])).then_inc(s_ln2, 16)
            for a in range(TT):
                for q in range(4):
                    cols = slice(q * 512, (q + 1) * 512)
                    sp.wait_ge(out_ready, 4 * a + q + 1)
                    sp.dma_start(out_d[a * P:(a + 1) * P, cols], acc[:, a, cols]).then_inc(s_out, 16)
            sp.wait_ge(s_out, 16 * 4 * TT)

        @block.gpsimd
        def _(pool):
            pool.memset(eps[:, :], EPS).then_inc(s_ones, 1)
            pool.memset(ones[:, :], 1.0).then_inc(s_ones, 1)
            pool.memset(cond_pad[:, :], 0.0).then_inc(s_pad, 1)
            pool.wait_ge(s_sguw, 16)
            w3 = sgu_wT[:, :].rearrange("p (g t) -> p g t", g=G)
            pool.affine_select(out=w3, in_=w3, compare_op=ALU.is_ge, fill=0.0, base=0,
                               pattern=[[0, G], [1, P]], channel_multiplier=-1).then_inc(causal, 1)

        def sum_bank(x, a, c):
            spare = psum[4] if x == 4 else psum[EXTRA[x][2]]
            four = (psum[6], psum[7], psum[4] if strips(x) == 4 else psum[5], spare)
            if strips(x) == 4:
                if a is None:
                    return four[c][:, :].rearrange("p (a n) -> p a n", a=TT)
                return four[c][:, a * 256:(a + 1) * 256]
            return four[2 * a + c][:, :]

        def joined(eng, name, count, extra, total):
            def level(n):
                xs = LEVELS[n]
                with eng.If(count > EXTRA[xs[0]][0]):
                    for x in xs:
                        extra(x)
                    eng.sem_inc(extra_end[name], 1)
                    if n + 1 < len(LEVELS):
                        level(n + 1)
                        eng.sem_inc(extra_end[name], 1)
                with eng.Else():
                    if total:
                        for x in EXTRA:
                            if x >= xs[0]:
                                total(x)
                    eng.sem_inc(extra_end[name], 1)
            level(0)

        def bank_of(x, n):
            return psum[n] if x == 0 else psum[EXTRA[x][2]]

        def expert_pe(pe, mm, g, le, count):
            ne = g * GRP + le

            def tokens(x, k):
                return xe[:, k, le * CAP:(le + 1) * CAP] if x == 0 else xx[x][:, k, :]

            def gate_up(x, j, half):
                w = slot(NFRONT + le * E_UNITS + 2 * j + half).rearrange("p (k u n) -> p k u n", k=8, u=2)
                n, m = P // strips(x), 512 // strips(x)
                for k in range(8):
                    for c in range(strips(x)):
                        last = nc.tensor.matmul(bank_of(x, j)[n * c:n * c + n, 0:2 * m], tokens(x, 8 * half + k),
                                                w[:, k, :, m * c:m * c + m],
                                                start=(half == 0 and k == 0), stop=(half == 1 and k == 7),
                                                tile_position=(0, n * c), skip_group_check=True)
                return last

            def down(x, q, ks):
                w = slot(NFRONT + le * E_UNITS + 4 + q).rearrange("p (k n) -> p k n", k=8)
                n, m = P // strips(x), 1024 // strips(x)
                for k in ks:
                    for c in range(strips(x)):
                        last = nc.tensor.matmul(bank_of(x, q)[n * c:n * c + n, 0:m], hidT[x][:, k, :],
                                                w[:, k, m * c:m * c + m], start=(k == 0), stop=(k == 7),
                                                tile_position=(0, n * c), skip_group_check=True)
                return last

            def turn(src, blocks=2):
                for b in range(blocks):
                    last = nc.tensor.transpose(psum[5][:, b * P:(b + 1) * P], src[:, b * P:(b + 1) * P], ident)
                return last

            def scatter(bank, x, y, c, a):
                n = P // strips(x)
                return nc.tensor.matmul(bank, back[x][n * c:n * c + n, a, :], y[n * c:n * c + n, :],
                                        start=True, stop=True, tile_position=(n * c, 0))

            def extra(sec):
                def run(x):
                    xp, xa, xd = x_pe[x], x_act[x], x_dve[x]
                    R, C = rounds(x), strips(x)
                    n = P // C
                    own = bank_of(x, 0)

                    def p(event):
                        return ne * pe_count(x, "all") + pe_count(x, event)

                    def a_(event):
                        return ne * act_count(x, "all") + act_count(x, event)

                    def d(event):
                        return ne * dve_count(x, "all") + dve_count(x, event)

                    if sec == "A":
                        if x == 4:
                            pe.wait_ge(m_taken[1], g * BANK_JOBS + 4 * (le + 1) + 1)
                        pe.wait_ge(xd, ne * dve_count(x, "all") + 1)
                        for q in range(R):
                            if q:
                                pe.wait_ge(xd, ne * dve_count(x, "all") + 1 + 2 * q)
                            for a in range(TT):
                                for c in range(C):
                                    col = c * (D // C) + q * 512
                                    last = nc.tensor.matmul(own[n * c:n * c + n, :], hotx[:, a, 0:n],
                                                            x1[:, a, col:col + 512], start=(a == 0), stop=(a == TT - 1),
                                                            tile_position=(0, n * c), skip_group_check=True)
                            last.then_inc(xp, 1)
                            pe.wait_ge(xa, ne * act_count(x, "all") + q + 1)
                            for i in range(4):
                                last = nc.tensor.transpose(own[:, i * P:(i + 1) * P], passing[:, i * P:(i + 1) * P],
                                                           ident)
                            last.then_inc(xp, 1)
                        turn(hotwx.rearrange("p a n -> p (a n)")).then_inc(xp, 1)
                        pe.wait_ge(xa, a_("oneT"))
                        pe.wait_ge(xd, d("tokens"))
                        gate_up(x, 0, 0)
                        pe.wait_ge(xp, p("oneT"))
                    elif sec == "B":
                        gate_up(x, 0, 1).then_inc(xp, 1)
                    elif sec == "C":
                        pe.wait_ge(xd, d("h0"))
                        gate_up(x, 1, 0)
                        turn(hidx[x], R).then_inc(xp, 1)
                        pe.wait_ge(xa, a_("t0"))
                    elif sec == "D":
                        gate_up(x, 1, 1).then_inc(xp, 1)
                    else:
                        q = int(sec == "F")
                        if x == 3:
                            pe.wait_ge(x_dve[2], ne * dve_count(2, "all") + dve_count(2, "all" if q else "s0"))
                        if q == 1:
                            pe.wait_ge(xd, d("s0"))
                        if q == 0:
                            pe.wait_ge(xd, d("h1"))
                            pe.wait_ge(t_taken, ne * 3 + 3)
                            turn(hidx[x], R).then_inc(xp, 1)
                            pe.wait_ge(xa, a_("all"))
                        down(x, q, range(8)).then_inc(xp, 1)
                        pe.wait_ge(xd, d("y1" if q else "y0"))
                        if q == 0:
                            for b in range(2):
                                pe.wait_ge(m_taken[b], g * BANK_JOBS + 4 * (le + 1) + 1)
                        for a in range(TT):
                            for c in range(C):
                                last = scatter(sum_bank(x, a, c), x, passing[:, 0:1024 // C], c, a)
                        last.then_inc(xp, 1)
                        if C == 2:
                            pe.wait_ge(xd, d("all" if q else "s0"))
                return run

            def extras(sec):
                joined(pe, "pe", count, extra(sec),
                       (lambda x: pe.sem_inc(x_pe[x], pe_count(x, "all"))) if sec == "F" else None)

            t = le * E_UNITS
            if le == 0:
                for b in range(2):
                    pe.wait_ge(m_taken[b], g * BANK_JOBS + 5)
            pe.wait_ge(hotw_ready, ne + 1)
            pe.wait_ge(t_taken, ne * 3 + 1)
            turn(hotw.rearrange("p a n -> p (a n)")).then_inc(t_full, 1)
            pe.wait_ge(t_taken, ne * 3 + 2)
            e_unit_loaded(pe, g, t)
            extras("A")
            pe.wait_ge(y_ready, ne * 2 + 1)
            gate_up(0, 0, 0).then_inc(used_ac, 1)
            e_unit_loaded(pe, g, t + 1)
            extras("B")
            gate_up(0, 0, 1).then_inc(h_full, 1)
            e_unit_loaded(pe, g, t + 2)
            extras("C")
            pe.wait_ge(y_ready, ne * 2 + 2)
            gate_up(0, 1, 0).then_inc(used_ac, 1)
            pe.wait_ge(hid_ready, ne * 2 + 1)
            turn(hid[0]).then_inc(t_full, 1)
            e_unit_loaded(pe, g, t + 3)
            extras("D")
            gate_up(0, 1, 1).then_inc(h_full, 1)
            e_unit_loaded(pe, g, t + 4)
            extras("E")
            pe.wait_ge(t_taken, ne * 3 + 3)
            down(0, 0, range(4))
            pe.wait_ge(hid_ready, ne * 2 + 2)
            turn(hid[1]).then_inc(t_full, 1)
            pe.wait_ge(t_taken, ne * 3 + 4)
            down(0, 0, range(4, 8)).then_inc(y_full, 1)
            e_unit_loaded(pe, g, t + 5)
            extras("F")
            down(0, 1, range(8)).then_inc(y_full, 1)
            pe.wait_ge(extras_added, ne + 1)
            for q in range(2):
                pe.wait_ge(y_ready, ne * 2 + 3 + q)
                for a in range(TT):
                    for c in range(2):
                        pe.wait_ge(m_taken[c], g * BANK_JOBS + 4 * (le + 1) + 1 + 2 * q + a)
                        scatter(psum[6 + c][:, :], 0, ysb[q], c, a).then_inc(m_full[c], 1)

        @block.tensor
        def _(pe):
            def mm(out, lhsT, rhs, start, stop):
                return nc.tensor.matmul(out, lhsT, rhs, start=start, stop=stop)

            def ada_step(a):
                m, j = ADA_UNITS[a]
                b = a - ADA_FIRST
                src = ada_row[a % 2]
                pe.wait_ge(ada_acc, a + 1)
                if 1 <= a <= ADA_FIRST:
                    pe.wait_ge(ada_out, a)
                elif a > ADA_FIRST:
                    pe.wait_ge(ada_outa, b)
                pick = ident[0:MOD * 4, 4 * m + j:4 * m + j + 1]
                if m in (G1, G2):
                    mm(psum[7][:, :], ones[:, :], src, True, False)
                    last = mm(psum[7][:, :], pick.to_broadcast([MOD * 4, P]), ada_bias[0:MOD * 4, :], False, True)
                else:
                    for c in range(4):
                        cols = slice(c * P, (c + 1) * P)
                        mm(psum[7][:, c:c + 1], src[:, cols], ones[:, 0:1], True, False)
                        last = mm(psum[7][:, c:c + 1], ada_bias[0:MOD * 4, cols], pick, False, True)
                last.then_inc(ada_sum, 1)

            def ada_multiply(a):
                n = AT["ada", a]
                unit_loaded(pe, n)
                if a >= 1:
                    pe.wait_ge(ada_acc, a)
                w = slot(n).rearrange("p (k n) -> p k n", n=UW)
                for k in range(KC):
                    c = k % 4
                    last = nc.tensor.matmul(psum[6][32 * c:32 * c + 32, :], cond_pad[:, 32 * k:32 * k + 32],
                                            w[:, k, :], start=(k < 4), stop=(k >= KC - 4), tile_position=(0, 32 * c))
                last.then_inc(ada_mm, 1)

            pe.wait_ge(s_cond, 2)
            ada_multiply(0)
            pe.wait_ge(s_ones, 2)
            pe.wait_ge(s_const, 32)
            ada_step(0)
            ada_multiply(1)
            ada_step(1)
            pe.wait_ge(s_rel, 32)
            pe.wait_ge(s_relone, 1)
            mm(psum[5][0:H, 0:TOE], rel[:, :], buckets, True, True).then_inc(s_toep, 1)
            pe.wait_ge(s_toer, 1)
            for r in range(4):
                unit_loaded(pe, AT["rows", r])
                wv, wz = row_parts(AT["rows", r])
                for i in range(BY_ROWS):
                    w = wz if i == 2 else wv[:, :, i * UW:(i + 1) * UW]
                    for m in range(TT):
                        if r < 3 and (i, m) == (2, 0):
                            ada_multiply(2 * r + 2)
                        if r < 3 and (i, m) == (2, 1):
                            ada_step(2 * r + 2)
                        for kk in range(4):
                            if i == 0 and m == 0:
                                pe.wait_ge(xm_ready, 4 * r + kk + 1)
                            last = mm(psum[job_bank(JOB[i, m])][:, :], xmT[:, 4 * r + kk, m * P:(m + 1) * P],
                                      w[:, kk, :], r == 0 and kk == 0, r == 3 and kk == 3)
                        if r == 3:
                            last.then_inc(job_full, 1)
                        elif m == TT - 1 and i > 0:
                            last.then_inc(rows_used, 1)
                if r < 3:
                    ada_multiply(2 * r + 3)
                    ada_step(2 * r + 3)

            def part(i, m, h):
                kind, j = W_UNITS[i]
                n, job = AT[("w", i)], JOB[i, m]
                bank = psum[job_bank(job)]
                if m == 0 and h == 0:
                    unit_loaded(pe, n)
                    if i == W_UNITS.index(("branch", 0)):
                        pe.wait_ge(o_taken, H)
                        pe.wait_ge(mix_taken, 4)
                    if kind == "out" and j == 0:
                        pe.wait_ge(mix_ready, KC)
                if h == 0 and job >= 4:
                    pe.wait_ge(dve_emptied if by_dve(job - 4) else act_emptied, evictions(job - 4))
                w = slot(n).rearrange("p (k n) -> p k n", n=UW)
                if kind == "branch":
                    src = attT if h == 0 else uT
                    for k in range(8):
                        last = mm(bank[:, h * T:(h + 1) * T], w[:, 8 * h + k, m * P:(m + 1) * P], src[:, k, :],
                                  k == 0, k == 7)
                elif kind in ("v", "z", "out"):
                    src = mixT if kind == "out" else xmT
                    for k in range(8 * h, 8 * h + 8):
                        last = mm(bank[:, :], src[:, k, m * P:(m + 1) * P], w[:, k, :], k == 0, k == KC - 1)
                else:
                    c = 2 * m + h
                    for k in range(KC):
                        last = mm(bank[:, h * T:(h + 1) * T], w[:, k, c * P:(c + 1) * P], xmT[:, k, :],
                                  k == 0, k == KC - 1)
                if h == 1:
                    last.then_inc(job_full, 1)

            def att(s):
                if s < H:
                    if s == 0:
                        pe.wait_ge(act_emptied, 14)
                    else:
                        pe.wait_ge(sc_taken, s)
                    mm(psum[4][:, 0:P], qT[:, s, 0:P], kT[:, s, 0:P], True, True)
                    mm(psum[4][:, P:3 * P], qT[:, s, P:T], kT[:, s, :], True, True).then_inc(sc_full, 1)
                if 1 <= s <= H:
                    pe.wait_ge(p_norm, s)
                    if s >= 2:
                        pe.wait_ge(pt_taken, s - 1)
                    pr = prob[(s - 1) % 2]
                    for b in range(3):
                        last = nc.tensor.transpose(psum[5][:, b * P:(b + 1) * P], pr[:, b * P:(b + 1) * P], ident)
                    last.then_inc(pt_full, 1)
                if s >= 2:
                    h = s - 2
                    pe.wait_ge(pt_taken, h + 1)
                    if h >= 1:
                        pe.wait_ge(o_taken, h)
                    ptb = pTs[h % 2]
                    mm(psum[6][:, 0:T], v[:, 0, h * P:(h + 1) * P], ptb[:, 0:T], True, False)
                    mm(psum[6][:, P:T], v[:, 1, h * P:(h + 1) * P], ptb[:, T:3 * P], False, True).then_inc(o_full, 1)

            def mix(m):
                a = m // 2
                if m == 0:
                    pe.wait_ge(z_ready, 1)
                    pe.wait_ge(causal, 1)
                    pe.wait_ge(pt_taken, H)
                    pe.wait_ge(o_taken, H)
                    pe.wait_ge(sc_taken, H)
                if m == 3:
                    pe.wait_ge(mix_taken, 1)
                bank = psum[4 + m % 3]
                for q in range(4):
                    grp = 4 * (m % 2) + q
                    out = bank[:, q * P:(q + 1) * P]
                    mm(out, zv[:, a, grp * P:(grp + 1) * P], sgu_wT[:, grp * P:(grp + 1) * P], True, False)
                    last = mm(out, ident[0:G, grp:grp + 1].to_broadcast([G, P]), sgu_bias[:, :], False, True)
                last.then_inc(mix_full, 1)

            def turn_x1(a, m):
                pe.wait_ge(x1_ready, 4 * a + m + 1)
                if a > 0:
                    pe.wait_ge(xt_taken[0], m + 1)
                for kk in range(4):
                    k = 4 * m + kk
                    last = nc.tensor.transpose(psum[4 + m][:, kk * P:(kk + 1) * P], x1[:, a, k * P:(k + 1) * P], ident)
                last.then_inc(xt_full, 1)

            def logits(a, m):
                if (a, m) == (1, 3):
                    pe.wait_ge(xt_taken[1], 1)
                else:
                    pe.wait_ge(xt_taken[0], 4 * a + m + 1)
                for k in range(4 * m, 4 * m + 4):
                    last = mm(psum[a][0:NE, 0:P], router_w[:, k * NE:(k + 1) * NE], hmT[:, k, a * P:(a + 1) * P],
                              k == 0, k == KC - 1)
                if m == 3:
                    last.then_inc(lg_full, 1)

            for step in SCHEDULE:
                if step == ("part", NW - 1, 1, 1):
                    for m in range(3):
                        turn_x1(0, m)
                if step[0] == "part":
                    part(*step[1:])
                elif step[0] == "att":
                    att(step[1])
                elif step[0] == "ada":
                    ada_step(step[1])
                elif step[0] == "mix":
                    mix(step[1])
            turn_x1(0, 3)
            pe.wait_ge(s_router, 48)
            for m in range(4):
                logits(0, m)
            for m in range(3):
                turn_x1(1, m)
            logits(1, 0)
            turn_x1(1, 3)
            for m in range(1, 4):
                logits(1, m)
            pe.wait_ge(lg_copied, TT)
            for a in range(TT):
                last = nc.tensor.transpose(psum[4][:, a * NE:(a + 1) * NE], lgT[:, a * P:(a + 1) * P], ident[0:NE, 0:NE])
            last.then_inc(lg_turned, 1)
            pe.wait_ge(mask_ready, 1)
            mm(psum[5][:, 0:NE], upper, mask[:, 0:NE], True, True)
            mm(psum[5][:, NE:2 * NE], ones[:, :], mask[:, 0:NE], True, False)
            mm(psum[5][:, NE:2 * NE], upper, mask[:, NE:2 * NE], False, True)
            mm(psum[5][:, 2 * NE:3 * NE], ones[:, :], mask[:, 0:NE], True, False)
            mm(psum[5][:, 2 * NE:3 * NE], ones[:, :], mask[:, NE:2 * NE], False, True).then_inc(place_full, 1)

            pe.wait_ge(routed, 1)
            with pe.Fori(0, NE // GRP) as g:
                pe.wait_ge(hot_ready, g + 1)
                for m in range(KC // 2):
                    b = m % 2
                    pe.wait_ge(m_taken[b], g * BANK_JOBS + m // 2 + 1)
                    for kk in range(2):
                        k = 2 * m + kk
                        for a in range(TT):
                            last = mm(psum[6 + b][:, kk * T:(kk + 1) * T], x1[:, a, k * P:(k + 1) * P],
                                      hot[:, a, :, :].rearrange("p e s -> p (e s)"), a == 0, a == TT - 1)
                    last.then_inc(m_full[b], 1)
                for le in range(GRP):
                    count = pe.value_load(counts[0:1, bass.ds(g * GRP + le, 1)], min_val=0, max_val=T)
                    expert_pe(pe, mm, g, le, count)

        def expert_act(act, g, le, count):
            ne = g * GRP + le

            def take_turned(x, j):
                C = strips(x)
                out = hidT[x][:, 4 * j:4 * j + 4, :].rearrange("p (c a) s -> p a c s", c=C)
                return act.activation(out, psum[5][:, 0:4 // C * P].rearrange("p (a c s) -> p a c s", a=4 // C, c=C),
                                      ACT.Copy)

            def extra(sec):
                def run(x):
                    xp, xa = x_pe[x], x_act[x]
                    own = bank_of(x, 0)

                    def p(event):
                        return ne * pe_count(x, "all") + pe_count(x, event)

                    def a_(event):
                        return ne * act_count(x, "all") + act_count(x, event)

                    if sec == "A":
                        for q in range(rounds(x)):
                            act.wait_ge(xp, ne * pe_count(x, "all") + 2 * q + 1)
                            act.activation(passing, own[:, :], ACT.Copy).then_inc(xa, 1)
                        act.wait_ge(xp, p("oneT"))
                        act.activation(back[x].rearrange("p a t -> p (a t)"), psum[5][:, 0:2 * P], ACT.Copy)\
                           .then_inc(xa, 1)
                        act.wait_ge(xa, a_("oneT"))
                    elif sec in "BD":
                        event = "h0" if sec == "B" else "h1"
                        act.wait_ge(xp, p(event))
                        act.activation(hidx[x], own[:, 0:512 // strips(x)], ACT.Silu).then_inc(xa, 1)
                        act.wait_ge(xa, a_(event))
                    else:
                        act.wait_ge(xp, p("t0" if sec == "C" else "t1"))
                        take_turned(x, 0 if sec == "C" else 1).then_inc(xa, 1)
                        act.wait_ge(xa, a_("t0" if sec == "C" else "all"))
                return run

            def extras(sec):
                joined(act, "act", count, extra(sec),
                       (lambda x: act.sem_inc(x_act[x], act_count(x, "all"))) if sec == "E" else None)

            act.wait_ge(t_full, ne * 3 + 1)
            act.activation(back[0].rearrange("p a t -> p (a t)"), psum[5][:, 0:2 * P], ACT.Copy)\
               .then_inc(t_taken, 1)
            extras("A")
            for j, (one, two) in enumerate((("B", "C"), ("D", "E"))):
                extras(one)
                act.wait_ge(h_full, ne * 2 + 1 + j)
                act.activation(silu_g[j], psum[j][:, 0:256], ACT.Silu).then_inc(h_silu, 1)
                extras(two)
                act.wait_ge(t_full, ne * 3 + 2 + j)
                take_turned(0, j).then_inc(t_taken, 1)

        @block.scalar
        def _(act):
            def load(dst, src, s):
                act.dma_start(dst, src).then_inc(s, 16)

            load(rel[0:BUCKETS, :], rel_bias_d, s_rel)
            load(buckets, buckets_d, s_rel)
            load(square[:, :], square_d, s_const)
            load(ada_bias[0:MOD * 4, :], ada_b_d, s_const)
            for i in range(4):
                cols = slice(i * 4 * T, (i + 1) * 4 * T)
                load(region_a[:, cols], x_T_d[:, cols], s_xT)
            act.wait_ge(s_c, 16)
            act.activation(condT[:, :], cT[:, :], ACT.Silu).then_inc(s_cond, 1)
            act.wait_ge(s_pad, 1)
            act.activation(cond_pad[:, :].rearrange("p (k c) -> p k c", c=32)[:, :, 0], cT[:, :], ACT.Silu)\
               .then_inc(s_cond, 1)
            for a in range(ADA_FIRST):
                act.wait_ge(ada_mm, a + 1)
                if a >= 2:
                    act.wait_ge(ada_sum, a - 1)
                act.activation(ada_row[a % 2], psum[6][:, :], ACT.Copy).then_inc(ada_acc, 1)
                if a == 1:
                    act.wait_ge(s_toep, 1)
                    act.activation(toe_row, psum[5][0:H, 0:TOE], ACT.Copy).then_inc(s_toer, 1)
            act.wait_ge(s_toer, 1)
            load(toe_dram[:, :, :], toe_row.rearrange("h (o j) -> h o j", o=1).to_broadcast([H, P, TOE]), s_toed)
            load(sgu_wT[:, :], sgu_wT_d, s_sguw)
            load(sgu_g, sgu_g_d.to_broadcast([P, G * P]), s_sgubc)
            load(sgu_b, sgu_b_d.to_broadcast([P, G * P]), s_sgubc)
            load(sgu_bias[:, :], sgu_bias_d, s_sgubc)
            load(slots[:, :], slots_d, s_router)
            load(router_w[:, :].rearrange("p (k e) -> p k e", e=NE), router_w_d.rearrange("(k p) e -> p k e", p=P), s_router)
            load(router_b, router_b_d.to_broadcast([P, NE]), s_router)
            act.wait_ge(s_toed, 16)
            blocks = bass.AP(toe_dram[:, :, :].tensor, P - 1, [[TOE - 1, P], [P * TOE, H], [1, T]])
            load(toep, blocks, s_toe)

            def evict(i, m):
                kind, j = W_UNITS[i]
                job = JOB[i, m]
                act.wait_ge(job_full, job + 1)
                src = psum[job_bank(job)][:, :]
                pair = src.rearrange("p (c t) -> p c t", c=2)
                chunk = 4 * j + 2 * m
                if kind == "q":
                    ins = act.activation(qT[:, chunk:chunk + 2, :], pair, ACT.Copy)
                elif kind == "k":
                    ins = act.activation(kT[:, chunk:chunk + 2, :], pair, ACT.Copy)
                elif kind == "v":
                    ins = act.activation(v[:, m, j * UW:(j + 1) * UW], src, ACT.Copy)
                elif kind == "u":
                    ins = act.activation(uT[:, chunk:chunk + 2, :], pair, ACT.Gelu_apprx_tanh)
                elif kind == "z":
                    ins = act.activation(zv[:, m, j * UW:(j + 1) * UW], src, ACT.Gelu_apprx_tanh)
                else:
                    b = int(kind == "gate1")
                    if j == 0:
                        act.wait_ge(o_full, H)
                    else:
                        act.wait_ge(dve_emptied, 4 * j)
                    ins = act.activation(gates[:, 2 * m:2 * m + 2, b, :], pair, ACT.Sigmoid)
                ins.then_inc(act_emptied, 1)

            def ada_take(a):
                m, j = ADA_UNITS[a]
                act.wait_ge(ada_sum, a + 1)
                if m == G1:
                    ins = act.activation(g1b[:, j * UW:(j + 1) * UW], psum[7][:, :], ACT.Copy)
                elif m == G2:
                    c, q = j % 2, j // 2
                    half = slice(64 * c, 64 * c + 64)
                    act.activation(g2x[half, q * UW:(q + 1) * UW], psum[7][half, :], ACT.Copy)
                    for i in range(2):
                        strip = slice(64 * c + 32 * i, 64 * c + 32 * i + 32)
                        ins = act.activation(g2n[strip, q * 256:(q + 1) * 256], psum[7][strip, i * 256:(i + 1) * 256],
                                             ACT.Copy)
                else:
                    col = (2 if m == SC2 else 3) * KC + 4 * j
                    ins = act.activation(modcol[:, col:col + 4], psum[7][:, 0:4], ACT.Copy)
                ins.then_inc(ada_outa, 1)

            def att(s):
                if s < H:
                    pr = prob[s % 2]
                    act.wait_ge(s_max, s + 1)
                    act.activation(pr[:, 0:P], pr[:, 0:P], ACT.Exp, bias=nmax2[s % 2][:, 0:1],
                                   accum_out=rsum2[s % 2][:, 0:1])
                    act.activation(pr[:, P:3 * P], pr[:, P:3 * P], ACT.Exp, bias=nmax2[s % 2][:, 1:2],
                                   accum_out=rsum2[s % 2][:, 1:2]).then_inc(s_exp, 1)
                if s >= 2:
                    act.wait_ge(o_full, s - 1)
                    act.activation(attT[:, s - 2, :], psum[6][:, 0:T], ACT.Copy).then_inc(o_taken, 1)

            for i in range(BY_ROWS):
                for m in range(TT):
                    evict(i, m)
            for step in SCHEDULE:
                if step[0] == "part" and step[3] == 1 and not by_dve(JOB[step[1], step[2]]):
                    evict(step[1], step[2])
                elif step[0] == "att":
                    att(step[1])
                elif step[0] == "ada":
                    ada_take(step[1])
                elif step[0] == "norm":
                    act.wait_ge(z_var, 1)
                    act.activation(zrstd, zmv[:, :, 1], ACT.Sqrt, bias=eps[:, :]).then_inc(z_std, 1)
                if step == ("mix", 3):
                    act.wait_ge(sc_taken, H)
                    act.wait_ge(z_ready, 1)
                    load(x1, x_tok_d.rearrange("(a p) d -> p a d", p=P), s_x)
                    act.wait_ge(mix_full, 4)
                    load(ln1g, ln1_g_d.to_broadcast([P, D]), s_ln1)
            act.wait_ge(job_full, JOB[W_UNITS.index(("branch", 3)), 3] + 1)
            load(ln1b, ln1_b_d.to_broadcast([P, D]), s_ln1)

            def root(first, a):
                act.wait_ge(l_var, first + a + 1)
                act.activation(lrstd[:, a:a + 1], lmv[:, a, 1:2], ACT.Sqrt, bias=eps[:, :]).then_inc(l_std, 1)

            def modulate(a, m):
                act.wait_ge(xt_full, 4 * a + m + 1)
                for kk in range(4):
                    k = 4 * m + kk
                    ins = act.activation(hmT[:, k, a * P:(a + 1) * P], psum[4 + m][:, kk * P:(kk + 1) * P], ACT.Identity,
                                         scale=modcol[:, 2 * KC + k:2 * KC + k + 1],
                                         bias=modcol[:, 3 * KC + k:3 * KC + k + 1])
                ins.then_inc(xt_taken[0], 1)

            def copy_logits(a):
                act.wait_ge(lg_full, a + 1)
                act.activation(lgT[:, a * P:(a + 1) * P], psum[a][0:NE, 0:P], ACT.Copy).then_inc(lg_copied, 1)

            root(0, 0)
            act.wait_ge(s_sc2, 1)
            for m in range(4):
                modulate(0, m)
            root(0, 1)
            copy_logits(0)
            for m in range(3):
                modulate(1, m)
            copy_logits(1)
            act.wait_ge(lg_sub, 1)
            act.activation(aff, aff, ACT.Exp).then_inc(lg_exp, 1)
            for a in range(TT):
                act.activation(acc[:, a, :], x1[:, a, :], ACT.Copy, scale=ALPHA).then_inc(acc_ready, 1)
            act.wait_ge(routed, 1)

            with act.Fori(0, NE // GRP) as g:
                for m in range(KC // 2):
                    b = m % 2
                    act.wait_ge(m_full[b], g * BANK_JOBS + m // 2 + 1)
                    for kk in range(2):
                        k = 2 * m + kk
                        ins = act.activation(xe[:, k, :], psum[6 + b][:, kk * T:(kk + 1) * T], ACT.Identity,
                                             scale=modcol[:, 2 * KC + k:2 * KC + k + 1],
                                             bias=modcol[:, 3 * KC + k:3 * KC + k + 1])
                    ins.then_inc(m_taken[b], 1)
                for le in range(GRP):
                    count = act.value_load(counts[0:1, bass.ds(g * GRP + le, 1)], min_val=0, max_val=T)
                    expert_act(act, g, le, count)
            for a in range(TT):
                root(TT, a)

        @block.vector
        def _(dve):
            links = [0]

            def link(ins):
                links[0] += 1
                ins.then_inc(link_dve, 1)
                dve.wait_ge(link_dve, links[0])

            link(dve.memset(rel[BUCKETS:BUCKETS + 1, :], 1.0))
            dve.sem_inc(s_relone, 1)
            dve.wait_ge(s_cond, 1)

            def scaled(x, gamma, beta, a, first, done):
                def columns(t, q):
                    return t[..., q * 512:(q + 1) * 512]

                def centred(q):
                    part = columns(x[:, a, :], q)
                    return dve.scalar_tensor_tensor(out=part, in0=part, scalar=lmv[:, a, 0:1], in1=columns(gamma, q),
                                                    op0=ALU.subtract, op1=ALU.mult)

                dve.wait_ge(l_var, first + a + 1)
                centred(0)
                dve.wait_ge(l_std, first + a + 1)
                link(dve.reciprocal(lrstd[:, a:a + 1], lrstd[:, a:a + 1]))
                for q in range(4):
                    part = columns(x[:, a, :], q)
                    dve.scalar_tensor_tensor(out=part, in0=part, scalar=lrstd[:, a:a + 1], in1=columns(beta, q),
                                             op0=ALU.mult, op1=ALU.add).then_inc(done, 1)
                    if q < 3:
                        link(centred(q + 1))

            def ada_take(a):
                m, j = ADA_UNITS[a]
                dve.wait_ge(ada_sum, a + 1)
                dst = modcol[:, (0 if m == SC1 else KC) + 4 * j:(0 if m == SC1 else KC) + 4 * j + 4]
                ins = dve.tensor_scalar(dst, psum[7][:, 0:4], 1.0 if m == SC1 else 0.0, None, ALU.add)
                ins.then_inc(ada_out, 1)
                if m == SH1:
                    dve.wait_ge(ada_out, a + 1)
                    dve.wait_ge(s_xT, 64)
                    for k in range(4 * j, 4 * j + 4):
                        dve.tensor_scalar(xmT[:, k, :], xmT[:, k, :], modcol[:, k:k + 1],
                                          modcol[:, KC + k:KC + k + 1], ALU.mult, ALU.add).then_inc(xm_ready, 1)

            def ada_part(a, ks):
                dst = ada_row[a % 2]
                if ks[0] == 0:
                    unit_loaded(dve, AT["ada", a])
                    if a >= 2:
                        dve.wait_ge(ada_sum, max(a - 1, ADA_FIRST))
                w = slot(AT["ada", a]).rearrange("p (k n) -> p k n", n=UW)
                for k in ks:
                    if k == 0:
                        ins = dve.tensor_scalar(dst, w[:, 0, :], condT[:, 0:1], None, ALU.mult)
                    else:
                        ins = dve.scalar_tensor_tensor(out=dst, in0=w[:, k, :], scalar=condT[:, k:k + 1], in1=dst,
                                                       op0=ALU.mult, op1=ALU.add)
                    if k < KC - 1:
                        link(ins)
                    else:
                        ins.then_inc(ada_acc, 1)

            for a in range(ADA_FIRST):
                ada_take(a)

            def att(s):
                if s < H:
                    pr = prob[s % 2]
                    if s == 0:
                        dve.wait_ge(s_toe, 16)
                    dve.wait_ge(sc_full, s + 1)
                    if s >= 2:
                        dve.wait_ge(pt_full, s - 1)
                    dve.scalar_tensor_tensor(out=pr[:, 0:P], in0=psum[4][:, 0:P], scalar=QSCALE,
                                             in1=toep[:, s, P:T], op0=ALU.mult, op1=ALU.add)
                    ins = dve.scalar_tensor_tensor(out=pr[:, P:3 * P], in0=psum[4][:, P:3 * P], scalar=QSCALE,
                                                   in1=toep[:, s, :], op0=ALU.mult, op1=ALU.add)
                    ins.then_inc(sc_taken, 1)
                    dve.wait_ge(sc_taken, s + 1)
                    dve.tensor_reduce(nmax2[s % 2][:, 0:1], pr[:, 0:P], AX_X, ALU.max, negate=True)
                    dve.tensor_reduce(nmax2[s % 2][:, 1:2], pr[:, P:3 * P], AX_X, ALU.max, negate=True)\
                       .then_inc(s_max, 1)
                if 1 <= s <= H:
                    dve.wait_ge(pt_full, s)
                    if s >= 3:
                        dve.wait_ge(o_full, s - 2)
                    dve.tensor_copy(pTs[(s - 1) % 2], psum[5][:, 0:3 * P]).then_inc(pt_taken, 1)
                if s < H:
                    dve.wait_ge(s_exp, s + 1)
                    link(dve.reciprocal(rinv, rsum2[s % 2]))
                    dve.tensor_scalar(pr[:, 0:P], pr[:, 0:P], rinv[:, 0:1], None, ALU.mult)
                    ins = dve.tensor_scalar(pr[:, P:3 * P], pr[:, P:3 * P], rinv[:, 1:2], None, ALU.mult)
                    ins.then_inc(p_norm, 1)

            def gating_norm():
                dve.wait_ge(act_emptied, 20)
                dve.wait_ge(s_sgubc, 48)
                for a in range(TT):
                    for q in range(G):
                        ins = dve.bn_stats(zstat[:, a * G + q, :], zv[:, a, q * P:(q + 1) * P])
                link(ins)
                for n in range(TT * G):
                    ins = dve.bn_aggr(zmv[:, n, :], zstat[:, n, :])
                ins.then_inc(z_var, 1)
                dve.wait_ge(z_std, 1)
                link(dve.reciprocal(zrstd, zrstd))
                for a in range(TT):
                    for q in range(G):
                        n = a * G + q
                        z = zv[:, a, q * P:(q + 1) * P]
                        ins = dve.tensor_scalar(z, z, zmv[:, n, 0:1], zrstd[:, n:n + 1], ALU.subtract, ALU.mult)
                link(ins)
                for a in range(TT):
                    ins = dve.tensor_tensor(zv[:, a, :], zv[:, a, :], sgu_g, ALU.mult)
                link(ins)
                for a in range(TT):
                    ins = dve.tensor_tensor(zv[:, a, :], zv[:, a, :], sgu_b, ALU.add)
                ins.then_inc(z_ready, 1)

            def gated(m):
                a, half = m // 2, m % 2
                dve.wait_ge(mix_full, m + 1)
                u = uT[:, 4 * half:4 * half + 4, a * P:(a + 1) * P]
                dve.tensor_tensor(u, u, psum[4 + m % 3][:, :].rearrange("p (q t) -> p q t", q=4), ALU.mult)\
                   .then_inc(mix_taken, 1)

            def evict(i, m):
                kind, j = W_UNITS[i]
                job = JOB[i, m]
                dve.wait_ge(job_full, job + 1)
                bank = psum[job_bank(job)][:, :]
                t = tmp[job % 2]
                if kind == "branch":
                    dve.wait_ge(act_emptied, evictions(JOB[i - 1, m // 2]))
                    ins = dve.tensor_tensor(t, bank, gates[:, m, :, :].rearrange("p b t -> p (b t)"), ALU.mult)
                    ins.then_inc(dve_emptied, 1)
                    dve.wait_ge(dve_emptied, evictions(job))
                    dve.tensor_tensor(mixT[:, 4 * j + m, :], t[:, 0:T], t[:, T:2 * T], ALU.add).then_inc(mix_ready, 1)
                else:
                    cols = slice(j * UW, (j + 1) * UW)
                    if j == 0 and m == 0:
                        dve.wait_ge(s_x, 16)
                    dve.tensor_tensor(t, bank, g1b[:, cols], ALU.mult).then_inc(dve_emptied, 1)
                    dve.wait_ge(dve_emptied, evictions(job))
                    link(dve.scalar_tensor_tensor(out=x1[:, m, cols], in0=x1[:, m, cols], scalar=ALPHA, in1=t,
                                                  op0=ALU.mult, op1=ALU.add))
                    ins = dve.bn_stats(lstat[:, m, j, :], x1[:, m, cols])
                    if j == 3:
                        link(ins)
                        if m == 0:
                            dve.wait_ge(s_ln1, 32)
                        dve.bn_aggr(lmv[:, m, :], lstat[:, m, :, :].rearrange("p n s -> p (n s)")).then_inc(l_var, 1)
                        scaled(x1, ln1g, ln1b, m, 0, x1_ready)

            for step in SCHEDULE:
                if step[0] == "part" and step[3] == 1 and by_dve(JOB[step[1], step[2]]):
                    evict(step[1], step[2])
                elif step[0] == "att":
                    att(step[1])
                elif step[0] == "adapart":
                    ada_part(*step[1:])
                elif step[0] == "norm":
                    gating_norm()
                elif step[0] == "mix":
                    gated(step[1])
                elif step == ("ada", len(ADA_UNITS) - 1):
                    dve.wait_ge(ada_outa, len(ADA_UNITS) - ADA_FIRST)
                    dve.tensor_scalar(modcol[:, 2 * KC:3 * KC], modcol[:, 2 * KC:3 * KC], 1.0, None, ALU.add)\
                       .then_inc(s_sc2, 1)
                    dve.memset(cmp_, 0.0)
                    link(dve.memset(gcmp, 0.0))

            def tiles(t, n):
                return t.rearrange("p (a e) -> p a e", e=n)

            dve.wait_ge(xt_full, 4 * TT)
            for kk in range(4):
                k = KC - 4 + kk
                ins = dve.tensor_scalar(hmT[:, k, P:T], psum[7][:, kk * P:(kk + 1) * P],
                                        modcol[:, 2 * KC + k:2 * KC + k + 1],
                                        modcol[:, 3 * KC + k:3 * KC + k + 1], ALU.mult, ALU.add)
            ins.then_inc(xt_taken[1], 1)
            dve.wait_ge(s_router, 48)
            dve.wait_ge(lg_turned, 1)
            lg = psum[4][:, 0:2 * NE]
            link(dve.tensor_tensor(tiles(aff, NE), tiles(lg, NE),
                                   router_b.rearrange("p (a e) -> p a e", a=1).to_broadcast([P, TT, NE]), ALU.add))
            link(dve.tensor_reduce(gsc[:, 0:TT], tiles(aff, NE), AX_X, ALU.max))
            for a in range(TT):
                ins = dve.tensor_scalar(aff[:, a * NE:(a + 1) * NE], aff[:, a * NE:(a + 1) * NE], gsc[:, a:a + 1],
                                        None, ALU.subtract)
            ins.then_inc(lg_sub, 1)
            dve.wait_ge(lg_exp, 1)
            link(dve.tensor_reduce(gsc[:, 0:TT], tiles(aff, NE), AX_X, ALU.add))
            link(dve.reciprocal(gsc[:, 2:2 + TT], gsc[:, 0:TT]))
            for a in range(TT):
                ins = dve.tensor_scalar(aff[:, a * NE:(a + 1) * NE], aff[:, a * NE:(a + 1) * NE],
                                        gsc[:, 2 + a:3 + a], None, ALU.mult)
            link(ins)

            def ranks(out, val, buf, n):
                val = val.rearrange("p (n j) -> p n j", j=4)
                c = buf.rearrange("p (n i j) -> p n i j", i=4, j=4)
                for i in range(4):
                    if i > 0:
                        ins = dve.tensor_tensor(c[:, :, i, 0:i], val[:, :, i:i + 1].to_broadcast([P, n, i]),
                                                val[:, :, 0:i], ALU.is_gt)
                    if i < 3:
                        ins = dve.tensor_tensor(c[:, :, i, i + 1:4], val[:, :, i:i + 1].to_broadcast([P, n, 3 - i]),
                                                val[:, :, i + 1:4], ALU.is_ge)
                link(ins)
                link(dve.tensor_reduce(out.rearrange("p (n j) -> p n j", j=4), c.rearrange("p n i j -> p n j i"),
                                       AX_X, ALU.add))

            ranks(rank, aff, cmp_, TT * NG)
            link(dve.tensor_scalar(sel, rank, 1.5, None, ALU.is_lt))
            link(dve.tensor_tensor(best, sel, aff, ALU.mult))
            link(dve.tensor_reduce(gsc, best.rearrange("p (n j) -> p n j", j=4), AX_X, ALU.add))
            ranks(grank, gsc, gcmp, TT)
            link(dve.tensor_scalar(grank, grank, 0.5, None, ALU.is_lt))
            in_best = grank.rearrange("p (n o) -> p n o", o=1).to_broadcast([P, TT * NG, 4])
            dve.tensor_tensor(mask.rearrange("p (n j) -> p n j", j=4), sel.rearrange("p (n j) -> p n j", j=4),
                              in_best, ALU.mult).then_inc(mask_ready, 1)
            link(dve.tensor_tensor(best.rearrange("p (n j) -> p n j", j=4), best.rearrange("p (n j) -> p n j", j=4),
                                   in_best, ALU.mult))
            link(dve.tensor_reduce(gsc[:, 0:TT], tiles(best, NE), AX_X, ALU.add))
            link(dve.reciprocal(gsc[:, 2:2 + TT], gsc[:, 0:TT]))
            for a in range(TT):
                ins = dve.tensor_scalar(wts[:, a * NE:(a + 1) * NE], best[:, a * NE:(a + 1) * NE],
                                        gsc[:, 2 + a:3 + a], None, ALU.mult)
            link(ins)
            dve.wait_ge(place_full, 1)
            link(dve.scalar_tensor_tensor(out=place, in0=psum[5][:, 0:2 * NE], scalar=-FAR, in1=mask,
                                          op0=ALU.add, op1=ALU.mult))
            link(dve.tensor_scalar(place, place, FAR, None, ALU.add))
            dve.tensor_copy(counts[:, :], psum[5][:, 2 * NE:3 * NE]).then_inc(routed, 1)
            dve.wait_ge(routed, 1)
            dve.wait_ge(acc_ready, TT)
            dve.sem_inc(y_ready, 2)
            dve.sem_inc(m_taken[0], 1)
            dve.sem_inc(m_taken[1], 1)
            dve.sem_inc(t_taken, 1)

            def slot_no(first, n, copies):
                return slots[:, first:first + n].rearrange("p (o s) -> p o s", o=1).to_broadcast([P, copies, n])

            with dve.Fori(0, NE // GRP) as g:
                def chosen(e, a):
                    return place.rearrange("p (a e) -> p a e", a=TT)[:, a, bass.ds(e, 1)]

                def weight(e, a):
                    return wts.rearrange("p (a e) -> p a e", a=TT)[:, a, bass.ds(e, 1)]

                for le in range(GRP):
                    for a in range(TT):
                        ins = dve.tensor_scalar(hot[:, a, le, :], slots[:, 0:CAP], chosen(g * GRP + le, a), None,
                                                ALU.is_equal)
                ins.then_inc(hot_ready, 1)
                for le in range(GRP):
                    count = dve.value_load(counts[0:1, bass.ds(g * GRP + le, 1)], min_val=0, max_val=T)
                    ne = g * GRP + le
                    for a in range(TT):
                        ins = dve.tensor_scalar(hotw[:, a, :].rearrange("p (c s) -> p c s", s=CAP),
                                                slot_no(0, CAP, 2), chosen(ne, a), weight(ne, a),
                                                ALU.is_equal, ALU.mult)
                    ins.then_inc(hotw_ready, 1)

                    def extra(sec):
                        def run(x):
                            xp, xa, xd = x_pe[x], x_act[x], x_dve[x]
                            R, C = rounds(x), strips(x)
                            first, n, _ = EXTRA[x]
                            own = bank_of(x, 0)

                            def p(event):
                                return ne * pe_count(x, "all") + pe_count(x, event)

                            def d(event):
                                return ne * dve_count(x, "all") + dve_count(x, event)

                            if sec == "A":
                                for a in range(TT):
                                    dve.tensor_scalar(hotx[:, a, 0:n], slots[:, first:first + n], chosen(ne, a), None,
                                                      ALU.is_equal)
                                    ins = dve.tensor_scalar(hotwx[:, a, :].rearrange("p (c s) -> p c s", s=n),
                                                            slot_no(first, n, C), chosen(ne, a), weight(ne, a),
                                                            ALU.is_equal, ALU.mult)
                                ins.then_inc(xd, 1)
                                for q in range(R):
                                    dve.wait_ge(xp, ne * pe_count(x, "all") + 2 * q + 2)

                                    def chunks(t):
                                        return t.rearrange("p (c q i) o -> p q i c o", c=C, q=R)[:, q]

                                    def col(m):
                                        cols = modcol[:, m * KC:(m + 1) * KC].rearrange("p (k o) -> p k o", o=1)
                                        return chunks(cols).to_broadcast([P, 4, C, n])

                                    dst = chunks(xx[x])
                                    dve.tensor_tensor(dst, own[:, :].rearrange("p (i c s) -> p i c s", i=4, c=C),
                                                      col(2), ALU.mult).then_inc(xd, 1)
                                    dve.wait_ge(xd, ne * dve_count(x, "all") + 2 * q + 2)
                                    ins = dve.tensor_tensor(dst, dst, col(3), ALU.add)
                                    ins.then_inc(xd, 1)
                                dve.wait_ge(xp, p("oneT"))
                                dve.wait_ge(xd, d("tokens"))
                            elif sec in "BD":
                                event = "h0" if sec == "B" else "h1"
                                dve.wait_ge(xa, ne * act_count(x, "all") + act_count(x, event))
                                m = 512 // C
                                dve.tensor_tensor(hidx[x], hidx[x], own[:, m:2 * m], ALU.mult).then_inc(xd, 1)
                                dve.wait_ge(xd, d(event))
                            else:
                                q = int(sec == "F")
                                m = 1024 // C
                                gate = (g2n if C == 4 else g2x)[:, q * m:(q + 1) * m]
                                dve.wait_ge(xp, p("y1" if q else "y0"))
                                dve.tensor_tensor(passing[:, 0:m], own[:, 0:m], gate, ALU.mult).then_inc(xd, 1)
                                dve.wait_ge(xp, p("all" if q else "s0"))
                                dst = acc[:, :, q * 1024:(q + 1) * 1024].rearrange("p a (c n) -> p a c n", c=C)
                                if C == 4:
                                    for c in range(C):
                                        both = sum_bank(x, None, c)
                                        ins = dve.tensor_tensor(dst[:, :, c, :], both, dst[:, :, c, :], ALU.add)
                                else:
                                    for a in range(TT):
                                        for c in range(C):
                                            ins = dve.tensor_tensor(dst[:, a, c, :], sum_bank(x, a, c), dst[:, a, c, :],
                                                                    ALU.add)
                                ins.then_inc(xd, 1)
                                dve.wait_ge(xd, d("all" if q else "s0"))
                        return run

                    def extras(sec):
                        joined(dve, "dve", count, extra(sec),
                               (lambda x: dve.sem_inc(x_dve[x], dve_count(x, "all"))) if sec == "F" else None)

                    def add(bank, q, a, c):
                        dst = acc[:, a, q * 1024 + c * 512:q * 1024 + (c + 1) * 512]
                        return dve.tensor_tensor(dst, bank[:, :], dst, ALU.add)

                    def scale(q):
                        dve.wait_ge(y_full, ne * 2 + 1 + q)
                        dve.tensor_tensor(ysb[q], psum[q][:, :], g2x[:, q * UW:(q + 1) * UW], ALU.mult)\
                           .then_inc(y_ready, 1)

                    extras("A")
                    for j, (one, two) in enumerate((("B", "C"), ("D", "E"))):
                        extras(one)
                        dve.wait_ge(h_silu, ne * 2 + 1 + j)
                        dve.tensor_tensor(hid[j], silu_g[j], psum[j][:, 256:512], ALU.mult).then_inc(hid_ready, 1)
                        if two == "E":
                            extras(two)
                    scale(0)
                    extras("F")
                    dve.sem_inc(extras_added, 1)
                    scale(1)
                    for q in range(2):
                        for a in range(TT):
                            for c in range(2):
                                dve.wait_ge(m_full[c], g * BANK_JOBS + 4 * (le + 1) + 2 * q + a + 1)
                                add(psum[6 + c], q, a, c).then_inc(m_taken[c], 1)
                    for c in range(2):
                        dve.wait_ge(m_taken[c], g * BANK_JOBS + 4 * (le + 2) + 1)

            dve.wait_ge(s_ln2, 32)
            for a in range(TT):
                for q in range(4):
                    ins = dve.bn_stats(lstat[:, a, q, :], acc[:, a, q * 512:(q + 1) * 512])
                link(ins)
                dve.bn_aggr(lmv[:, a, :], lstat[:, a, :, :].rearrange("p n s -> p (n s)")).then_inc(l_var, 1)
            for a in range(TT):
                scaled(acc, ln2g, ln2b, a, TT, out_ready)


_OUT = (1, T, D)


def kernel(**inputs):
    import numpy as np
    import concourse.bacc as bacc
    from concourse.bass_utils import run_bass_kernel_spmd

    a = {k: np.asarray(v) for k, v in inputs.items()}

    square = np.zeros((P, 2 * P), np.float32)
    square[:, :P] = np.eye(P)
    square[:, P:] = np.triu(np.ones((P, P)), 1)
    slots = np.broadcast_to(np.arange(T, dtype=np.float32), (P, T))
    buckets = np.zeros((BUCKETS + 1, TOE), np.float32)
    for j in range(TOE):
        dist = T - 1 - j
        times = sum(dist >= 0 and dist % d == 0 and dist <= w for w, d in PATTERNS)
        buckets[BUCKETS, j] = np.log(times) if times else -1e30
        if times:
            half = BUCKETS // 2
            far = half + int(np.log(np.float32(max(dist, 1)) / np.float32(half))
                             / np.float32(np.log(2048 / half)) * np.float32(BUCKETS - half))
            buckets[dist if dist < half else min(far, BUCKETS - 1), j] = 1.0

    row = lambda t: t.reshape(1, -1)
    arrays = {
        "x_tok": a["x"][0],
        "x_T": a["x"][0].T.reshape(KC, P, T).transpose(1, 0, 2).reshape(P, KC * T),
        "c_T": a["c"].reshape(KC, P).T,
        "rel_bias": a["rel_bias"],
        "router_w": a["router_w"],
        "router_b": row(a["router_b"]),
        "ada_w": a["ada_w"][0],
        "ada_b": a["ada_b"].reshape(MOD * 4, UW),
        "w_in": a["w_in"][0],
        "sgu_g": row(a["sgu_ln_g"]),
        "sgu_b": row(a["sgu_ln_b"]),
        "sgu_wT": a["sgu_w"][0].transpose(2, 0, 1).reshape(P, G * P),
        "sgu_bias": a["sgu_b"][0],
        "w_branch": a["w_branch"].reshape(D, D),
        "w_out": a["w_out"][0],
        "ln1_g": row(a["ln1_g"]), "ln1_b": row(a["ln1_b"]),
        "ln2_g": row(a["ln2_g"]), "ln2_b": row(a["ln2_b"]),
        "w_gate": a["exp_w_gate"][0], "w_up": a["exp_w_up"][0], "w_down": a["exp_w_down"][0],
        "square": square, "slots": slots, "buckets": buckets,
    }
    arrays = {k: np.ascontiguousarray(t) for k, t in arrays.items()}
    nc = bacc.Bacc("TRN2", target_bir_lowering=False, num_devices=1, dynamic_dma_scratch_size=1024)
    args = {k + "_d": nc.dram_tensor("in_" + k, t.shape, F32, kind="ExternalInput").ap() for k, t in arrays.items()}
    out = nc.dram_tensor("out", (T, D), F32, kind="ExternalOutput").ap()
    program(nc, out_d=out, **args)
    r = run_bass_kernel_spmd(nc, [{"in_" + k: t for k, t in arrays.items()}], core_ids=[0])
    return r.results[0]["out"].reshape(_OUT)
```
